# Optimizing a Trainium2 kernel written in Bass

```python
import math
import jax, jax.numpy as jnp
from jax import lax
import numpy as np

D_MODEL = 1024
BATCH = 1
SEQ = 256
DEPTH = 4

N_MIXERS = 3
N_MLA = (DEPTH + 2) // 3
N_MOBA = (DEPTH + 1) // 3
N_SSD = DEPTH // 3
NORM_EPS = 1e-6
NEG_INF = -1e30
MAX_POS_OFFSET = 4096

MLA_HEADS = 16
MLA_Q_RANK = 256
MLA_KV_RANK = 256
MLA_NOPE = 128
MLA_ROPE = 64
MLA_V = 128
ROPE_BASE = 10000.0
ATTN_QBLOCK = 128

MOBA_HEADS = 8
MOBA_HEAD_DIM = D_MODEL // MOBA_HEADS
MOBA_BLOCK = 256
MOBA_TOPK = 3
MOBA_QCHUNK = 16

REL_BUCKETS = 32
REL_MAX_DIST = 128

SSD_INNER = 2 * D_MODEL
SSD_HEAD_DIM = 64
SSD_HEADS = SSD_INNER // SSD_HEAD_DIM
SSD_GROUPS = 2
SSD_HEADS_PER_GROUP = SSD_HEADS // SSD_GROUPS
SSD_STATE = 128
SSD_CONV = 4
SSD_CONV_DIM = SSD_INNER + 2 * SSD_GROUPS * SSD_STATE
SSD_IN_DIM = SSD_INNER + SSD_CONV_DIM + SSD_HEADS
SSD_CHUNK = 128

MLP_HIDDEN = 4 * D_MODEL

kernel_name = 'hybrid_mla_moba_ssd_trunk'

def rmsnorm(x, g):
    xf = x.astype(jnp.float32)
    y = xf * lax.rsqrt(jnp.mean(xf * xf, axis=-1, keepdims=True) + NORM_EPS)
    return (y * g.astype(jnp.float32)).astype(x.dtype)

def rope_angles(positions):
    inv_freq = ROPE_BASE ** (-(jnp.arange(0, MLA_ROPE, 2, dtype=jnp.float32) / MLA_ROPE))
    ang = positions.astype(jnp.float32)[..., None] * inv_freq
    return jnp.cos(ang), jnp.sin(ang)

def apply_rope(x, cos, sin):
    x1, x2 = jnp.split(x.astype(jnp.float32), 2, axis=-1)
    return jnp.concatenate([x1 * cos - x2 * sin, x2 * cos + x1 * sin], axis=-1).astype(x.dtype)

def t5_bucket(dist):
    n = jnp.maximum(dist, 0)
    max_exact = REL_BUCKETS // 2
    nf = jnp.maximum(n, max_exact).astype(jnp.float32)
    large = max_exact + (jnp.log(nf / max_exact) / math.log(REL_MAX_DIST / max_exact)
                         * (REL_BUCKETS - max_exact)).astype(jnp.int32)
    large = jnp.minimum(large, REL_BUCKETS - 1)
    return jnp.where(n < max_exact, n, large)

def mla_mixer(h, positions, w_in, q_norm, w_uq, kv_norm, w_ukv, w_o):
    B, S, _ = h.shape
    proj = h @ w_in
    c_q, c_kv, k_pe = jnp.split(proj, [MLA_Q_RANK, MLA_Q_RANK + MLA_KV_RANK], axis=-1)
    q = (rmsnorm(c_q, q_norm) @ w_uq).reshape(B, S, MLA_HEADS, MLA_NOPE + MLA_ROPE)
    q_nope, q_pe = jnp.split(q, [MLA_NOPE], axis=-1)
    kv = (rmsnorm(c_kv, kv_norm) @ w_ukv).reshape(B, S, MLA_HEADS, MLA_NOPE + MLA_V)
    k_nope, v = jnp.split(kv, [MLA_NOPE], axis=-1)
    cos, sin = rope_angles(positions)
    q_pe = apply_rope(q_pe, cos[:, :, None], sin[:, :, None])
    k_pe = apply_rope(k_pe, cos, sin)
    scale = (MLA_NOPE + MLA_ROPE) ** -0.5
    nqb = S // ATTN_QBLOCK
    key_idx = jnp.arange(S)

    def block(args):
        qn, qp, start = args
        logits = (jnp.einsum('bqhd,bkhd->bhqk', qn, k_nope)
                  + jnp.einsum('bqhr,bkr->bhqk', qp, k_pe)).astype(jnp.float32) * scale
        q_idx = start + jnp.arange(ATTN_QBLOCK)
        causal = key_idx[None, :] <= q_idx[:, None]
        p = jax.nn.softmax(jnp.where(causal, logits, NEG_INF), axis=-1)
        return jnp.einsum('bhqk,bkhd->bqhd', p.astype(v.dtype), v)

    def to_blocks(t):
        return jnp.moveaxis(t.reshape(B, nqb, ATTN_QBLOCK, *t.shape[2:]), 1, 0)

    out = lax.map(block, (to_blocks(q_nope), to_blocks(q_pe), jnp.arange(nqb) * ATTN_QBLOCK))
    out = jnp.moveaxis(out, 0, 1).reshape(B, S, MLA_HEADS * MLA_V)
    return out @ w_o

def moba_mixer(h, w_qkv, w_o, rel_bias):
    B, S, _ = h.shape
    H, Dh, BLK = MOBA_HEADS, MOBA_HEAD_DIM, MOBA_BLOCK
    s_pad = -(-S // BLK) * BLK
    nb = s_pad // BLK
    k_sel = min(MOBA_TOPK, nb)
    qkv = (h @ w_qkv).reshape(B, S, 3, H, Dh)
    qkv = jnp.pad(qkv, ((0, 0), (0, s_pad - S), (0, 0), (0, 0), (0, 0)))
    q = jnp.moveaxis(qkv[:, :, 0], 1, 2)
    k = jnp.moveaxis(qkv[:, :, 1], 1, 2)
    v = jnp.moveaxis(qkv[:, :, 2], 1, 2)
    kb = k.reshape(B, H, nb, BLK, Dh)
    vb = v.reshape(B, H, nb, BLK, Dh)
    k_mean = jnp.mean(kb.astype(jnp.float32), axis=3)
    gate = jnp.einsum('bhsd,bhnd->bhsn', q.astype(jnp.float32), k_mean)
    q_blk = jnp.arange(s_pad) // BLK
    past = jnp.arange(nb)[None, :] < q_blk[:, None]
    _, sel = lax.top_k(jnp.where(past, gate, NEG_INF), k_sel)
    sel_valid = sel < q_blk[:, None]
    bias_tab = rel_bias.T
    scale = Dh ** -0.5
    nc = s_pad // MOBA_QCHUNK
    gather_blocks = jax.vmap(jax.vmap(lambda blocks, idx: blocks[idx]))
    head_idx = jnp.arange(H)[None, :, None, None, None]

    def chunk(args):
        qc, sc, vc, c = args
        start = c * MOBA_QCHUNK
        q_idx = start + jnp.arange(MOBA_QCHUNK)
        k_g = gather_blocks(kb, sc)
        v_g = gather_blocks(vb, sc)
        key_idx = sc[..., None] * BLK + jnp.arange(BLK)
        bias_g = bias_tab[head_idx, t5_bucket(q_idx[:, None, None] - key_idx)]
        logit_g = jnp.einsum('bhqd,bhqjkd->bhqjk', qc, k_g).astype(jnp.float32) * scale + bias_g
        logit_g = jnp.where(vc[..., None], logit_g, NEG_INF).reshape(B, H, MOBA_QCHUNK, k_sel * BLK)
        own = (start // BLK) * BLK
        k_o = lax.dynamic_slice_in_dim(k, own, BLK, axis=2)
        v_o = lax.dynamic_slice_in_dim(v, own, BLK, axis=2)
        dist_o = q_idx[:, None] - (own + jnp.arange(BLK))[None, :]
        logit_o = (jnp.einsum('bhqd,bhkd->bhqk', qc, k_o).astype(jnp.float32) * scale
                   + bias_tab[:, t5_bucket(dist_o)])
        logit_o = jnp.where(dist_o >= 0, logit_o, NEG_INF)
        p = jax.nn.softmax(jnp.concatenate([logit_g, logit_o], axis=-1), axis=-1).astype(v.dtype)
        p_g = p[..., :k_sel * BLK].reshape(B, H, MOBA_QCHUNK, k_sel, BLK)
        p_o = p[..., k_sel * BLK:]
        return (jnp.einsum('bhqjk,bhqjkd->bhqd', p_g, v_g)
                + jnp.einsum('bhqk,bhkd->bhqd', p_o, v_o))

    def to_chunks(t):
        return jnp.moveaxis(t.reshape(B, H, nc, MOBA_QCHUNK, *t.shape[3:]), 2, 0)

    out = lax.map(chunk, (to_chunks(q), to_chunks(sel), to_chunks(sel_valid), jnp.arange(nc)))
    out = out.transpose(1, 0, 3, 2, 4).reshape(B, s_pad, H * Dh)[:, :S]
    return out @ w_o

def causal_depthwise_conv(x, w, b):
    C = x.shape[-1]
    y = lax.conv_general_dilated(x, w[:, None, :], window_strides=(1,),
                                 padding=[(SSD_CONV - 1, 0)],
                                 dimension_numbers=('NWC', 'WIO', 'NWC'),
                                 feature_group_count=C)
    return y + b

def ssd_scan(xh, dt, a, bm, cm):
    B, S = xh.shape[:2]
    L = SSD_CHUNK
    nc = S // L

    def chunks(t):
        return t.reshape(B, nc, L, *t.shape[2:])

    x_dt = chunks(xh * dt[..., None])
    a_cs = jnp.cumsum(chunks(dt * a), axis=2)
    bc = chunks(bm)
    cc = chunks(cm)
    tril = jnp.arange(L)[:, None] >= jnp.arange(L)[None, :]
    seg = a_cs[:, :, :, None] - a_cs[:, :, None, :]
    decay_in = jnp.exp(jnp.where(tril[None, None, :, :, None, None], seg, NEG_INF))
    cb = jnp.einsum('bclgn,bcsgn->bclsg', cc, bc)
    y_diag = jnp.einsum('bclsg,bclsgr,bcsgrp->bclgrp', cb, decay_in, x_dt)
    decay_out = jnp.exp(a_cs[:, :, -1:] - a_cs)
    states = jnp.einsum('bclgn,bclgr,bclgrp->bcgrpn', bc, decay_out, x_dt)
    chunk_decay = jnp.exp(a_cs[:, :, -1])

    def step(state, inp):
        st, dec = inp
        return dec[..., None, None] * state + st, state

    init = jnp.zeros_like(states[:, 0])
    _, prev = lax.scan(step, init, (jnp.moveaxis(states, 1, 0), jnp.moveaxis(chunk_decay, 1, 0)))
    prev = jnp.moveaxis(prev, 0, 1)
    y_off = jnp.einsum('bclgn,bcgrpn,bclgr->bclgrp', cc, prev, jnp.exp(a_cs))
    return (y_diag + y_off).reshape(B, S, *xh.shape[2:])

def ssd_mixer(h, w_in, conv_w, conv_b, dt_bias, a_log, d_skip, norm_w, w_out):
    B, S, _ = h.shape
    proj = h @ w_in
    z, xbc, dt = jnp.split(proj, [SSD_INNER, SSD_INNER + SSD_CONV_DIM], axis=-1)
    xbc = jax.nn.silu(causal_depthwise_conv(xbc, conv_w, conv_b))
    xs, bm, cm = jnp.split(xbc, [SSD_INNER, SSD_INNER + SSD_GROUPS * SSD_STATE], axis=-1)
    dt = jax.nn.softplus(dt.astype(jnp.float32) + dt_bias.astype(jnp.float32))
    a = -jnp.exp(a_log.astype(jnp.float32))
    grp = (SSD_GROUPS, SSD_HEADS_PER_GROUP)
    xh = xs.reshape(B, S, *grp, SSD_HEAD_DIM)
    y = ssd_scan(xh, dt.reshape(B, S, *grp), a.reshape(grp),
                 bm.reshape(B, S, SSD_GROUPS, SSD_STATE), cm.reshape(B, S, SSD_GROUPS, SSD_STATE))
    y = y + d_skip.astype(jnp.float32).reshape(*grp, 1) * xh
    g = y * jax.nn.silu(z.astype(jnp.float32)).reshape(B, S, *grp, SSD_HEAD_DIM)
    g = g.reshape(B, S, SSD_GROUPS, SSD_INNER // SSD_GROUPS)
    g = g * lax.rsqrt(jnp.mean(g * g, axis=-1, keepdims=True) + NORM_EPS)
    g = (g.reshape(B, S, SSD_INNER) * norm_w.astype(jnp.float32)).astype(h.dtype)
    return g @ w_out

def sq_relu_mlp(h, w1, w2):
    a = jax.nn.relu(h @ w1)
    return (a * a) @ w2

def setup_inputs(seed: int = 0) -> dict:
    key = jax.random.key(seed)
    ks = iter(jax.random.split(key, 40))
    f32 = jnp.float32
    out_scale = (2 * DEPTH) ** -0.5

    def dense(shape, fan_in, scale=1.0):
        return jax.random.normal(next(ks), shape, f32) * (scale * fan_in ** -0.5)

    def gain(shape):
        return 1.0 + 0.05 * jax.random.normal(next(ks), shape, f32)

    x = jax.random.normal(next(ks), (BATCH, SEQ, D_MODEL), f32)
    offsets = jax.random.randint(next(ks), (BATCH, 1), 0, MAX_POS_OFFSET, dtype=jnp.int32)
    positions = offsets + jnp.arange(SEQ, dtype=jnp.int32)[None, :]
    u = jax.random.uniform(next(ks), (N_SSD, SSD_HEADS), f32)
    dt0 = jnp.exp(u * (math.log(0.1) - math.log(0.001)) + math.log(0.001))
    return {
        'x': x,
        'positions': positions,
        'norm_mix': gain((DEPTH, D_MODEL)),
        'norm_mlp': gain((DEPTH, D_MODEL)),
        'norm_final': gain((D_MODEL,)),
        'rel_bias': 0.2 * jax.random.normal(next(ks), (REL_BUCKETS, MOBA_HEADS), f32),
        'mla_w_in': dense((N_MLA, D_MODEL, MLA_Q_RANK + MLA_KV_RANK + MLA_ROPE), D_MODEL),
        'mla_q_norm': gain((N_MLA, MLA_Q_RANK)),
        'mla_w_uq': dense((N_MLA, MLA_Q_RANK, MLA_HEADS * (MLA_NOPE + MLA_ROPE)), MLA_Q_RANK),
        'mla_kv_norm': gain((N_MLA, MLA_KV_RANK)),
        'mla_w_ukv': dense((N_MLA, MLA_KV_RANK, MLA_HEADS * (MLA_NOPE + MLA_V)), MLA_KV_RANK),
        'mla_w_o': dense((N_MLA, MLA_HEADS * MLA_V, D_MODEL), MLA_HEADS * MLA_V, out_scale),
        'moba_w_qkv': dense((N_MOBA, D_MODEL, 3 * D_MODEL), D_MODEL),
        'moba_w_o': dense((N_MOBA, D_MODEL, D_MODEL), D_MODEL, out_scale),
        'ssd_w_in': dense((N_SSD, D_MODEL, SSD_IN_DIM), D_MODEL),
        'ssd_conv_w': dense((N_SSD, SSD_CONV, SSD_CONV_DIM), SSD_CONV),
        'ssd_conv_b': 0.02 * jax.random.normal(next(ks), (N_SSD, SSD_CONV_DIM), f32),
        'ssd_dt_bias': dt0 + jnp.log(-jnp.expm1(-dt0)),
        'ssd_a_log': jnp.log(jax.random.uniform(next(ks), (N_SSD, SSD_HEADS), f32, 1.0, 16.0)),
        'ssd_d': gain((N_SSD, SSD_HEADS)),
        'ssd_norm': gain((N_SSD, SSD_INNER)),
        'ssd_w_out': dense((N_SSD, SSD_INNER, D_MODEL), SSD_INNER, out_scale),
        'mlp_w1': dense((DEPTH, D_MODEL, MLP_HIDDEN), D_MODEL),
        'mlp_w2': dense((DEPTH, MLP_HIDDEN, D_MODEL), MLP_HIDDEN, out_scale),
    }

def reference(x, positions, norm_mix, norm_mlp, norm_final, rel_bias,
              mla_w_in, mla_q_norm, mla_w_uq, mla_kv_norm, mla_w_ukv, mla_w_o,
              moba_w_qkv, moba_w_o,
              ssd_w_in, ssd_conv_w, ssd_conv_b, ssd_dt_bias, ssd_a_log, ssd_d, ssd_norm, ssd_w_out,
              mlp_w1, mlp_w2):
    for i in range(DEPTH):
        kind, j = i % N_MIXERS, i // N_MIXERS
        h = rmsnorm(x, norm_mix[i])
        if kind == 0:
            m = mla_mixer(h, positions, mla_w_in[j], mla_q_norm[j], mla_w_uq[j],
                          mla_kv_norm[j], mla_w_ukv[j], mla_w_o[j])
        elif kind == 1:
            m = moba_mixer(h, moba_w_qkv[j], moba_w_o[j], rel_bias)
        else:
            m = ssd_mixer(h, ssd_w_in[j], ssd_conv_w[j], ssd_conv_b[j], ssd_dt_bias[j],
                          ssd_a_log[j], ssd_d[j], ssd_norm[j], ssd_w_out[j])
        x = x + m.astype(x.dtype)
        x = x + sq_relu_mlp(rmsnorm(x, norm_mlp[i]), mlp_w1[i], mlp_w2[i]).astype(x.dtype)
    return rmsnorm(x, norm_final)


_drawn_inputs = setup_inputs


def setup_inputs(seed=0):
    import zlib

    import numpy as np

    out = dict(_drawn_inputs(seed))
    spreads = {}
    factors = {'rel_bias': 4.562,
     'mla_q_norm': 8.0,
     'mla_kv_norm': 7.177,
     'ssd_conv_b': 7.2,
     'ssd_d': 4.799,
     'ssd_norm': 3.825}
    for name, (base, spread) in spreads.items():
        noise = np.random.default_rng([zlib.crc32(name.encode()), seed]).standard_normal(out[name].shape)
        drawn = base * np.exp(spread * noise) if base else spread * noise
        out[name] = __import__('jax').numpy.asarray(drawn.astype(out[name].dtype))
    for name, factor in factors.items():
        out[name] = (out[name] * factor).astype(out[name].dtype)
    return out
```

```python
import math
from contextlib import ExitStack

import numpy as np

import concourse.bass as bass
from concourse import mybir

F32 = mybir.dt.float32
F32R = mybir.dt.float32r
I32 = mybir.dt.int32
ALU = mybir.AluOpType
ACT = mybir.ActivationFunctionType
AX = mybir.AxisListType

P = 128
SEQ = 256
T = SEQ // P
DM = 1024
KD = DM // P
DEPTH = 4
EPS = 1e-6
NEG = -1e30
HID = 4 * DM
CH = 256
NCH = HID // CH
SLOTS = 4
UNIT = 2048
AHEAD = 3

MLA_H, NOPE, ROPE, VD, QR, KVR = 16, 128, 64, 128, 256, 256
MLA_GRP = 4
MLA_SCALE = (NOPE + ROPE) ** -0.5
MOBA_H, MOBA_D = 8, 128
MOBA_SCALE = MOBA_D ** -0.5
BUCKETS, MAX_DIST = 32, 128

SSD_IN, SSD_HD, SSD_H, SSD_G, SSD_N, SSD_CONV = 2048, 64, 32, 2, 128, 4
SSD_XBC = SSD_IN + 2 * SSD_G * SSD_N
SSD_HG = SSD_H // SSD_G
ZT = SSD_IN // P

TWO_PI_A = 6.28125
TWO_PI_B = float(np.float32(round((2 * math.pi - 6.28125) * 2 ** 20) / 2 ** 20))
TWO_PI_C = float(np.float32(2 * math.pi - 6.28125 - TWO_PI_B))
ROUND_MAGIC = 1.5 * 2 ** 23
PI_IN = 3.1415925


def shape_constants():
    i = np.arange(P)
    tri = np.where(i[None, :] <= i[:, None], 0.0, NEG).astype(np.float32)
    mask = np.concatenate([tri, np.zeros((P, P), np.float32), tri], axis=1)
    inv = np.power(np.float32(10000.0), -(np.arange(0, ROPE, 2, dtype=np.float32) / np.float32(ROPE)))
    onehot = np.zeros((BUCKETS + 1, 384), np.float32)
    for m in range(384):
        dist = 255 - m
        if dist < 0:
            onehot[BUCKETS, m] = NEG
            continue
        half = BUCKETS // 2
        large = half + int(np.float32(np.log(np.float32(max(dist, half)) / np.float32(half)))
                           / np.float32(math.log(MAX_DIST / half)) * np.float32(BUCKETS - half))
        onehot[dist if dist < half else min(large, BUCKETS - 1), m] = 1.0
    upper = (i[None, :] >= i[:, None]).astype(np.float32)
    return {"c_ident": np.eye(P, dtype=np.float32), "c_mask": mask, "c_invfreq": inv.astype(np.float32)[None, :],
            "c_onehot": onehot, "c_upper": upper}


class Jobs:

    def __init__(self, bank_ready, bank_free):
        self.bank_ready, self.bank_free = bank_ready, bank_free
        self.at = {}
        self.last = 3
        self.n_ready, self.n_free = [0] * 4, [0] * 4
        self.prev_freed = [None] * 4

    def add(self, key, bank=None, ready=None, freed=None):
        b = (self.last + 1) % 4 if bank is None else bank
        self.last = b
        if ready is None:
            self.n_ready[b] += 1
            ready = (self.bank_ready[b], self.n_ready[b])
        if freed is None:
            self.n_free[b] += 1
            freed = (self.bank_free[b], self.n_free[b])
        assert key not in self.at, key
        self.at[key] = (b, ready, freed, self.prev_freed[b])
        self.prev_freed[b] = freed


def build(nc, A, out, stages):
    ctx = ExitStack()
    with ctx:
        def sb(name, shape, dt=F32, c=ctx):
            return c.enter_context(nc.sbuf_tensor(name, shape, dt))

        def sem(name):
            return ctx.enter_context(nc.semaphore(name))

        kinds = [s[0] for s in stages]
        NN = len(stages) + 1

        raw = sb("raw", [P, SLOTS, UNIT])
        whi = sb("whi", [P, SLOTS, UNIT], F32R)
        wlo = sb("wlo", [P, SLOTS, UNIT], F32R)
        x = sb("x", [P, T, DM])
        xn = sb("xn", [P, T, DM])
        gbc = sb("gbc", [P, DM])
        hhi = sb("hhi", [P, KD, SEQ], F32R)
        hlo = sb("hlo", [P, KD, SEQ], F32R)
        ident = sb("ident", [P, P])
        mask = sb("mask", [P, 384])
        junk = sb("junk", [P, DM])
        ssq = sb("ssq", [P, NN * T])
        ms = sb("ms", [P, NN * T])
        rstd = sb("rstd", [P, NN * T])
        neghalf = sb("neghalf", [P, 4])

        acc = [[ctx.enter_context(nc.psum_tensor(f"acc{t}{h}", [P, 512], F32)) for h in range(2)] for t in range(T)]
        bank = [ctx.enter_context(nc.psum_tensor(f"bank{b}", [P, 512], F32)) for b in range(4)]

        raw_loaded = [sem(f"raw_loaded{s}") for s in range(SLOTS)]
        w_hi_done = [sem(f"w_hi_done{s}") for s in range(SLOTS)]
        w_split = [sem(f"w_split{s}") for s in range(SLOTS)]
        w_used = [sem(f"w_used{s}") for s in range(SLOTS)]
        bank_ready = [sem(f"bank_ready{b}") for b in range(4)]
        bank_free = [sem(f"bank_free{b}") for b in range(4)]
        consts = sem("consts")
        x_loaded = sem("x_loaded")
        x_ready = sem("x_ready")
        gain_loaded = sem("gain_loaded")
        ssq_done = sem("ssq_done")
        ms_done = sem("ms_done")
        rstd_done = sem("rstd_done")
        xn_done = sem("xn_done")
        pool_const = sem("pool_const")
        h_hi_done = sem("h_hi_done")
        acc_done = sem("acc_done")
        relu_done = sem("relu_done")
        usq_done = sem("usq_done")
        uhi_done = sem("uhi_done")
        ulo_done = sem("ulo_done")
        out_stored = sem("out_stored")
        dve_seq = sem("dve_seq")

        csn = sb("csn", [P, T, 2, 2, ROPE // 2])
        qkvg = sb("qkvg", [P, 2, QR + KVR])
        c_ssq = sb("c_ssq", [P, 2, T, 2])
        c_ms = sb("c_ms", [P, 2, T, 2])
        c_rstd = sb("c_rstd", [P, 2, T, 2])
        mx = sb("mx", [P, 2, 2])
        nmx = sb("nmx", [P, 2, 2])
        rsum = sb("rsum", [P, 2, 2])
        rinv = sb("rinv", [P, 2, 2])

        crows = sb("crows", [P, P])
        drow = sb("drow", [ZT, 2])
        drows = sb("drows", [ZT, 2, SSD_HD])
        scol = sb("scol", [P, P + ZT])
        upper = sb("upper", [P, P])
        ones = sb("ones", [P, 1])
        headc = sb("headc", [SSD_H, 4])
        tokv = sb("tokv", [P, 6, SSD_H])
        g_ms = sb("g_ms", [P, SSD_G, T])
        g_rstd = sb("g_rstd", [P, SSD_G, T])

        with ExitStack() as stage:
            relu = sb("relu", [P, 2, 512], F32, stage)
            rsq = sb("rsq", [P, 2, 512], F32, stage)
            uhi = sb("uhi", [P, 2, 2, SEQ], F32R, stage)
            ulo = sb("ulo", [P, 2, 2, SEQ], F32R, stage)

        cn = xn[:, :, 0:QR + KVR]
        ropa, ropb, qp = (xn[:, :, n:n + 256].rearrange("p t (h d) -> p t h d", h=MLA_GRP) for n in (512, 768, 0))

        with ExitStack() as stage:
            S_sb = sb("S_sb", [P, 2, 384], F32, stage)
            P_sb = sb("P_sb", [P, 2, 384], F32, stage)
            PT_sb = sb("PT_sb", [P, 2, 384], F32, stage)
            ohi = sb("ohi", [P, 2, 2, SEQ], F32R, stage)
            olo = sb("olo", [P, 2, 2, SEQ], F32R, stage)
            qT = sb("qT", [P, 2, 4, SEQ], F32, stage)
            kT = sb("kT", [P, 2, 4, SEQ], F32, stage)
            v_sb = sb("v_sb", [P, 2, T, 512], F32, stage)
            with ExitStack() as mla:
                chi = sb("chi", [P, 4, SEQ], F32R, mla)
                clo = sb("clo", [P, 4, SEQ], F32R, mla)
                kp = sb("kp", [P, T, 2, ROPE], F32, mla)
                kpT = sb("kpT", [P, SEQ], F32, mla)
                qpT = sb("qpT", [P, 2, 2, SEQ], F32, mla)
                relx = sb("relx", [BUCKETS + 1, MOBA_H], F32, mla)
                onehot = sb("onehot", [BUCKETS + 1, 384], F32, mla)
                biasrow = sb("biasrow", [MOBA_H, 384], F32, mla)
                pos_i = sb("pos_i", [P, T], I32, mla)
                pos_f = sb("pos_f", [P, T], F32, mla)
                invf = sb("invf", [P, ROPE // 2], F32, mla)
                ang = sb("ang", [P, 4, T, ROPE // 2], F32, mla)
            bias = sb("bias", [P, MOBA_H, 384], F32, stage)

        dtv = xn[:].rearrange("p t (a n) -> p (t a) n", n=SEQ)
        xdt = xn[:, 0, :].rearrange("p (c n) -> p c n", c=T)
        dxdt = xn[:, 1, 0:512]
        prevT = xn[:, 1, 512:1024]
        y_sb = junk[:].rearrange("p (c n) -> p c n", c=T)
        with ExitStack() as stage:
            xsT = sb("xsT", [P, ZT, SEQ], F32, stage)
            BT = sb("BT", [P, SSD_G, SEQ], F32, stage)
            CT = sb("CT", [P, SSD_G, SEQ], F32, stage)
            Btok = sb("Btok", [P, SSD_G, P], F32, stage)
            cbm = sb("cbm", [P, SSD_G, T, P], F32, stage)
            dec = sb("dec", [P, 4, 8, P], F32, stage)
            with ExitStack() as conv_stage:
                cvin = sb("cvin", [P, 2, 2, SEQ + SSD_CONV - 1], F32, conv_stage)
                cacc = sb("cacc", [P, 2, 2, SEQ], F32, conv_stage)
            gy = sb("gy", [P, 2, 2, SEQ], F32, stage)
            sz = sb("sz", [P, 2, 2, SEQ], F32, stage)
            gsq = sb("gsq", [P, 512], F32, stage)
            gss = sb("gss", [P, 512], F32, stage)
            ghi = sb("ghi", [P, 2, 2, SEQ], F32R, stage)
            glo = sb("glo", [P, 2, 2, SEQ], F32R, stage)
        acs_dram = nc.dram_tensor("acs_rows", (SSD_H, SEQ), F32, kind="Internal").ap()
        if "ssd" in kinds:
            (ssd_loaded, upper_loaded, acs_stored, dt_abs, dt_exp, dt_u, dt_ln, dt_out, da_done, acs_done, dec_io,
             drows_done, conv_done, silu_done, dec_diff, dec_exp, dec_ready, dx_done, g_done, gsq_done, gadd_done,
             ghi_done, glo_done, gms_done, grstd_done, ssd_half, tokv_done) = (sem(n) for n in (
                 "ssd_loaded upper_loaded acs_stored dt_abs dt_exp dt_u dt_ln dt_out da_done acs_done dec_io "
                 "drows_done conv_done silu_done dec_diff dec_exp dec_ready dx_done g_done gsq_done gadd_done "
                 "ghi_done glo_done gms_done grstd_done ssd_half tokv_done").split())
            dec_loaded = [sem(f"dec_loaded{b}") for b in range(4)]

        at_sems = {L: {n: sem(f"{n}_{L}") for n in ("scores_masked", "exp_done", "probs_normed", "o_hi_done")}
                   for kind, L, i in stages if kind in ("mla", "moba")}
        mla_sems = {L: {n: sem(f"{n}_{L}") for n in
                        ("c_ssq_done", "c_ms_done", "c_rstd_done", "cn_done", "c_hi_done", "kp_done", "q_roped")}
                    for kind, L, i in stages if kind == "mla"}
        rope_loaded = sem("rope_loaded")
        qkvg_loaded = sem("qkvg_loaded")
        ang_done = sem("ang_done")
        sin_done = sem("sin_done")
        bias_dram = nc.dram_tensor("bias_rows", (MOBA_H, P, 384), F32, kind="Internal").ap()
        rel_loaded = sem("rel_loaded")
        brow_stored = sem("brow_stored")
        bias_loaded = sem("bias_loaded")

        units, first = [], {}

        def unit(key, a, b, *srcs):
            first[key] = len(units)
            units.append((a, b, srcs))

        def rows(w, lo, hi):
            return w[lo:hi, :].rearrange("(k p) n -> p k n", p=P)

        def cols(w, lo, hi):
            return w[:, lo:hi].rearrange("(k p) n -> p k n", p=P)

        def used(key):
            return w_used[first[key] % SLOTS], first[key] // SLOTS + 1

        jobs = Jobs(bank_ready, bank_free)

        def plan_norm(j):
            for t in range(T):
                for half in range(2):
                    jobs.add(("tr", j, t, half))

        def plan_mlp(L):
            w1, w2 = A["mlp_w1"][L], A["mlp_w2"][L]
            for c in range(NCH + 1):
                if c < NCH:
                    unit(("up", L, c), KD, CH, cols(w1, c * CH, (c + 1) * CH))
                    jobs.add(("up", L, c), ready=used(("up", L, c)))
                if c >= 1:
                    unit(("down", L, c - 1), 2, DM, rows(w2, (c - 1) * CH, c * CH))

        def plan_attn(L, heads, piece, w_o):
            for h in range(heads + 2):
                if h < heads:
                    jobs.add(("S", L, h))
                if 1 <= h <= heads:
                    jobs.add(("PT", L, h - 1))
                piece(h)
                if 1 <= h <= heads:
                    jobs.add(("O", L, h - 1))
                if h >= 3 and h % 2 == 1:
                    p = (h - 3) // 2
                    unit(("wo", L, p), 2, DM, rows(w_o, 2 * P * p, 2 * P * (p + 1)))

        def plan_mla_piece(L, i, g, q):
            if q == 0:
                unit(("uq", L, g), 2, MLA_GRP * (NOPE + ROPE),
                     cols(A["mla_w_uq"][i], MLA_GRP * (NOPE + ROPE) * g, MLA_GRP * (NOPE + ROPE) * (g + 1)))
                jobs.add(("qpe", L, g))
            if q == 1:
                jobs.add(("qn", L, g, 0))
                jobs.add(("qn", L, g, 1), ready=used(("uq", L, g)))
            if q == 2:
                unit(("ukv", L, g), 2, MLA_GRP * (NOPE + VD),
                     cols(A["mla_w_ukv"][i], MLA_GRP * (NOPE + VD) * g, MLA_GRP * (NOPE + VD) * (g + 1)))
                jobs.add(("qpT", L, g))
                jobs.add(("kn", L, g, 0))
                jobs.add(("kn", L, g, 1))
            if q == 3:
                jobs.add(("v", L, g, 0))
                jobs.add(("v", L, g, 1), ready=used(("ukv", L, g)))

        def plan_mla(L, i):
            w_in = A["mla_w_in"][i]
            M = mla_sems[L]
            unit(("cq", L), KD, QR, cols(w_in, 0, QR))
            unit(("ckv", L), KD, KVR, cols(w_in, QR, QR + KVR))
            unit(("kpe", L), KD, ROPE, cols(w_in, QR + KVR, QR + KVR + ROPE))
            jobs.add(("c", L, 0), freed=(M["cn_done"], 2))
            jobs.add(("c", L, 1), ready=used(("ckv", L)), freed=(M["cn_done"], 4))
            jobs.add(("kpe", L), ready=used(("kpe", L)))
            for t in range(T):
                jobs.add(("ct", L, t))
            jobs.add(("kpT", L))
            for q in range(4):
                plan_mla_piece(L, i, 0, q)
            plan_attn(L, MLA_H, lambda h: plan_mla_piece(L, i, h // 4 + 1, h % 4) if h < MLA_H - MLA_GRP else None,
                      A["mla_w_o"][i])

        def plan_moba_piece(L, h):
            w = A["moba_w_qkv"][0]
            if h % 2 == 0:
                p = h // 2
                unit(("mv", L, p), KD, 2 * MOBA_D, cols(w, 2 * DM + 256 * p, 2 * DM + 256 * (p + 1)))
                jobs.add(("mv", L, p), ready=used(("mv", L, p)))
            unit(("mqk", L, h), KD, 2 * MOBA_D, cols(w, P * h, P * (h + 1)), cols(w, DM + P * h, DM + P * (h + 1)))
            jobs.add(("mqk", L, h), ready=used(("mqk", L, h)))

        def plan_moba(L):
            plan_moba_piece(L, 0)
            plan_attn(L, MOBA_H, lambda h: plan_moba_piece(L, h + 1) if h < MOBA_H - 1 else None, A["moba_w_o"][0])

        def plan_ssd(L):
            w = A["ssd_w_in"][0]
            dt_col = SSD_IN + SSD_XBC
            unit("dt", KD, SSD_H, cols(w, dt_col, dt_col + SSD_H))
            jobs.add("dt", ready=used("dt"))
            jobs.add("scol")
            for n in range(10):
                c = SSD_IN + (SSD_IN + 256 * n if n < 2 else 256 * (n - 2))
                unit(("cv", n), KD, 256, cols(w, c, c + 256))
                jobs.add(("cv", n), ready=used(("cv", n)))
                if n == 4:
                    jobs.add("tokv")
                    jobs.add("cb")
                    jobs.add("Btok")
            for q in range(5):
                if q < 4:
                    jobs.add(("xT", q, 0))
                    jobs.add(("xT", q, 1))
                    for u in range(2):
                        n = 2 * q + u
                        unit(("z", n), KD, 256, cols(w, 256 * n, 256 * (n + 1)))
                        jobs.add(("z", n), ready=used(("z", n)))
                        if u == 0:
                            jobs.add(("st", q))
                    jobs.add(("yd", q, 0))
                    jobs.add(("yo", q))
                    jobs.add(("yd", q, 1))
                if q in (2, 4):
                    jobs.add(("ss", q // 2 - 1))
                if q:
                    for n in (2 * q - 2, 2 * q - 1):
                        unit(("so", L, n), 2, DM, rows(A["ssd_w_out"][0], 256 * n, 256 * (n + 1)))
                if q < 4:
                    jobs.add(("yT", q, 0))
                    jobs.add(("yT", q, 1))

        if "moba" in kinds:
            jobs.add("bias")
        stage_unit = {}
        for j, (kind, L, i) in enumerate(stages):
            plan_norm(j)
            stage_unit[len(units) + SLOTS] = j
            if kind == "mla":
                plan_mla(L, i)
            if kind == "moba":
                plan_moba(L)
            if kind == "mlp":
                plan_mlp(L)
            if kind == "ssd":
                plan_ssd(L)
        last_units = {}
        for j, (kind, L, i) in enumerate(stages):
            last_units[j] = {"mla": ("wo", L, MLA_H // 2 - 1), "moba": ("wo", L, MOBA_H // 2 - 1),
                             "mlp": ("down", L, NCH - 1), "ssd": ("so", L, 7)}[kind]

        raw_count, seen = [], [0] * SLOTS
        for n, (a, b, srcs) in enumerate(units):
            seen[n % SLOTS] += 16 * len(srcs)
            raw_count.append(seen[n % SLOTS])

        def hi_lo(key):
            a, b, _ = units[first[key]]
            s = first[key] % SLOTS
            return (whi[:, s, :a * b].rearrange("p (a b) -> p a b", a=a),
                    wlo[:, s, :a * b].rearrange("p (a b) -> p a b", a=a))

        def wait_unit(te, key):
            te.wait_ge(w_split[first[key] % SLOTS], first[key] // SLOTS + 1)

        def open_job(te, key):
            b, _, _, before = jobs.at[key]
            if before:
                te.wait_ge(*before)
            return bank[b]

        def job_ready(eng, key):
            eng.wait_ge(*jobs.at[key][1])
            return bank[jobs.at[key][0]]

        def ready(key):
            return jobs.at[key][1][0]

        def freed(key):
            return jobs.at[key][2][0]

        def job_copied(eng, key):
            eng.wait_ge(*jobs.at[key][2])

        split_to = {"act": 0, "dve": 0}

        def act_splits(act, key):
            while split_to["act"] < min(first[key] + AHEAD + 1, len(units)):
                n = split_to["act"]
                s, k = n % SLOTS, n // SLOTS
                e = units[n][0] * units[n][1]
                act.wait_ge(raw_loaded[s], raw_count[n])
                if k:
                    act.wait_ge(w_used[s], k)
                nc.scalar.activation(whi[:, s, :e], raw[:, s, :e], ACT.Copy).then_inc(w_hi_done[s], 1)
                split_to["act"] += 1

        def dve_splits(dve, key):
            while split_to["dve"] < min(first[key] + AHEAD + 1, len(units)):
                n = split_to["dve"]
                s, k = n % SLOTS, n // SLOTS
                e = units[n][0] * units[n][1]
                dve.wait_ge(w_hi_done[s], k + 1)
                nc.vector.tensor_tensor(wlo[:, s, :e], raw[:, s, :e], whi[:, s, :e].bitcast(F32),
                                        ALU.subtract).then_inc(w_split[s], 1)
                split_to["dve"] += 1

        dve_count = [0]

        def link(dve, ins):
            dve_count[0] += 1
            ins.then_inc(dve_seq, 1)
            dve.wait_ge(dve_seq, dve_count[0])

        def pair(hi, lo, *index):
            return hi[index], lo[index]

        def mm3(ps, lhs, rhs, start, stop):
            nc.tensor.matmul(ps, lhs[0], rhs[0], start=start, stop=False)
            nc.tensor.matmul(ps, lhs[0], rhs[1], start=False, stop=False)
            return nc.tensor.matmul(ps, lhs[1], rhs[0], start=False, stop=stop)

        def tok(t):
            return slice(t * P, (t + 1) * P)

        def x_value(j, t):
            return (j - 1) * 2 * T + 2 * (t + 1)

        def wait_x(eng, j, t):
            if j == 0:
                eng.wait_ge(x_loaded, 16)
            else:
                eng.wait_ge(x_ready, x_value(j, t))

        def act_sumsq(act, j):
            for t in range(T):
                wait_x(act, j, t)
                if j * T + t:
                    act.wait_ge(ssq_done, j * T + t)
                nc.scalar.activation(junk[:], x[:, t, :], ACT.Square,
                                     accum_out=ssq[:, j * T + t:j * T + t + 1]).then_inc(ssq_done, 1)

        def act_norm(act, j):
            act_sumsq(act, j)
            for t in range(T):
                for half in range(2):
                    ps = job_ready(act, ("tr", j, t, half))
                    nc.scalar.activation(hhi[:, 4 * half:4 * half + 4, tok(t)],
                                         ps[:].rearrange("p (k n) -> p k n", k=4), ACT.Copy).then_inc(h_hi_done, 1)

        def dve_scale_x(dve, j, t, deferred):
            c = j * T + t
            dve.wait_ge(gain_loaded, 16 * (j + 1))
            wait_x(dve, j, t)
            if deferred:
                nc.vector.tensor_tensor(xn[:, t, :], x[:, t, :], gbc[:], ALU.mult).then_inc(xn_done, 1)
                return
            dve.wait_ge(ssq_done, c + 1)
            nc.vector.tensor_scalar(ms[:, c:c + 1], ssq[:, c:c + 1], 1.0 / DM, EPS, ALU.mult, ALU.add).then_inc(ms_done, 1)
            dve.wait_ge(rstd_done, norm_index[j] * T + t + 1)
            nc.vector.scalar_tensor_tensor(out=xn[:, t, :], in0=x[:, t, :], scalar=rstd[:, c:c + 1],
                                           in1=gbc[:], op0=ALU.mult, op1=ALU.mult).then_inc(xn_done, 1)

        def dve_norm_lo(dve, j):
            for t in range(T):
                for half in range(2):
                    dve.wait_ge(h_hi_done, j * 4 + 2 * t + half + 1)
                    nc.vector.tensor_tensor(hlo[:, 4 * half:4 * half + 4, tok(t)],
                                            bank[jobs.at["tr", j, t, half][0]][:].rearrange("p (k n) -> p k n", k=4),
                                            hhi[:, 4 * half:4 * half + 4, tok(t)].bitcast(F32),
                                            ALU.subtract).then_inc(freed(("tr", j, t, half)), 1)

        def dve_square_rstd(dve, j):
            dve.wait_ge(ssq_done, (j + 1) * T)
            link(dve, nc.vector.tensor_scalar(ms[:, j * T:j * T + T], ssq[:, j * T:j * T + T], 1.0 / DM, EPS,
                                              ALU.mult, ALU.add))
            link(dve, nc.vector.reciprocal(rstd[:, j * T:j * T + T], ms[:, j * T:j * T + T]))

        def pool_norm(pool, j):
            for t in range(T):
                c = j * T + t
                pool.wait_ge(ms_done, norm_index[j] * T + t + 1)
                nc.gpsimd.tensor_tensor(rstd[:, c:c + 1], ms[:, c:c + 1], neghalf[:, 0:1], ALU.pow).then_inc(rstd_done, 1)

        def pe_norm(te, j):
            for t in range(T):
                te.wait_ge(xn_done, j * T + t + 1)
                for half in range(2):
                    ps = open_job(te, ("tr", j, t, half))
                    for k in range(4):
                        kk = 4 * half + k
                        mm = nc.tensor.transpose(ps[:, k * P:(k + 1) * P], xn[:, t, kk * P:(kk + 1) * P], ident[:])
                    mm.then_inc(ready(("tr", j, t, half)), 1)
            for t in range(T):
                for half in range(2):
                    job_copied(te, ("tr", j, t, half))

        def pe_out(te, key, lhs, first_unit, last_unit):
            wait_unit(te, key)
            wh, wl = hi_lo(key)
            for t in range(T):
                for k in range(2):
                    lh, ll = lhs[0][:, k, tok(t)], lhs[1][:, k, tok(t)]
                    for half in range(2):
                        n = slice(512 * half, 512 * half + 512)
                        nc.tensor.matmul(acc[t][half][:], lh, wh[:, k, n], start=first_unit and k == 0, stop=False)
                        nc.tensor.matmul(acc[t][half][:], lh, wl[:, k, n], start=False, stop=False)
                    for half in range(2):
                        n = slice(512 * half, 512 * half + 512)
                        mm = nc.tensor.matmul(acc[t][half][:], ll, wh[:, k, n], start=False,
                                              stop=last_unit and k == 1)
                if t == 0 and last_unit:
                    mm.then_inc(acc_done, 1)
            mm.then_inc(used(key)[0], 1)

        def dve_residual(dve, j, t):
            if t == 0:
                dve.wait_ge(acc_done, acc_rounds[j])
            else:
                dve.wait_ge(*used(last_units[j]))
            for half in range(2):
                n = slice(512 * half, 512 * half + 512)
                if stages[j][0] == "ssd":
                    ins = nc.vector.scalar_tensor_tensor(out=x[:, t, n], in0=acc[t][half][:],
                                                         scalar=g_rstd[:, 1, t:t + 1], in1=x[:, t, n],
                                                         op0=ALU.mult, op1=ALU.add)
                elif stages[j][0] == "mlp":
                    ins = nc.vector.scalar_tensor_tensor(out=x[:, t, n], in0=acc[t][half][:],
                                                         scalar=rstd[:, j * T + t:j * T + t + 1], in1=x[:, t, n],
                                                         op0=ALU.mult, op1=ALU.add)
                else:
                    ins = nc.vector.tensor_tensor(x[:, t, n], acc[t][half][:], x[:, t, n], ALU.add)
                ins.then_inc(x_ready, 1)

        norm_index, n_full = {}, 0
        for j in range(NN):
            if j == NN - 1 or stages[j][0] != "mlp":
                norm_index[j] = n_full
                n_full += 1
        acc_rounds, rounds = {}, 0
        for j, (kind, L, i) in enumerate(stages):
            rounds += 2 if kind == "ssd" else 1
            acc_rounds[j] = rounds

        def pe_mlp(te, j, L):
            h = (hhi, hlo)
            for c in range(NCH + 1):
                if c < NCH:
                    key = ("up", L, c)
                    wait_unit(te, key)
                    ps = open_job(te, key)
                    w = hi_lo(key)
                    for m in range(2):
                        for k in range(KD):
                            mm = mm3(ps[:, m * SEQ:(m + 1) * SEQ], (w[0][:, k, tok(m)], w[1][:, k, tok(m)]),
                                     (hhi[:, k, :], hlo[:, k, :]), k == 0, k == KD - 1)
                    mm.then_inc(used(key)[0], 1)
                if c >= 1:
                    te.wait_ge(ulo_done, mlp_base[L] + c)
                    s = (c - 1) % 2
                    pe_out(te, ("down", L, c - 1), (uhi[:, s], ulo[:, s]), c == 1, c == NCH)

        def act_mlp(act, j, L):
            for c in range(NCH):
                act_splits(act, ("up", L, c))
                n = mlp_base[L] + c
                if c >= 1:
                    act_splits(act, ("down", L, c - 1))
                ps = job_ready(act, ("up", L, c))
                nc.scalar.activation(relu[:, c % 2, :], ps[:], ACT.Relu).then_inc(freed(("up", L, c)), 1)
                act.wait_ge(usq_done, n + 1)
                if c >= 2:
                    act.wait_ge(*used(("down", L, c - 2)))
                nc.scalar.activation(uhi[:, c % 2].rearrange("p a b -> p (a b)"), rsq[:, c % 2, :],
                                     ACT.Copy).then_inc(uhi_done, 1)
            act_splits(act, ("down", L, NCH - 1))

        def dve_mlp(dve, j, L):
            dve_square_rstd(dve, j)
            for c in range(NCH):
                dve_splits(dve, ("up", L, c))
                n = mlp_base[L] + c
                if c >= 1:
                    dve_splits(dve, ("down", L, c - 1))
                job_copied(dve, ("up", L, c))
                nc.vector.tensor_tensor(rsq[:, c % 2, :], relu[:, c % 2, :], relu[:, c % 2, :],
                                        ALU.mult).then_inc(usq_done, 1)
                dve.wait_ge(uhi_done, n + 1)
                nc.vector.tensor_tensor(ulo[:, c % 2].rearrange("p a b -> p (a b)"), rsq[:, c % 2, :],
                                        uhi[:, c % 2].rearrange("p a b -> p (a b)").bitcast(F32),
                                        ALU.subtract).then_inc(ulo_done, 1)
            dve_splits(dve, ("down", L, NCH - 1))

        mlp_base, n_mlp = {}, 0
        for kind, L, i in stages:
            if kind == "mlp":
                mlp_base[L] = NCH * n_mlp
                n_mlp += 1

        def pe_attn(te, L, heads, qk, qk_waits, v_of, v_waits, piece):
            R = at_sems[L]
            for h in range(heads + 2):
                if h < heads:
                    for key in qk_waits(h):
                        job_copied(te, key)
                    ps = open_job(te, ("S", L, h))
                    for t in range(T):
                        dst = ps[:, 0:P] if t == 0 else ps[:, P:3 * P]
                        parts = qk(h)
                        for n, (q, k) in enumerate(parts):
                            mm = nc.tensor.matmul(dst, q[:, tok(t)], k[:, 0:(t + 1) * P], start=n == 0,
                                                  stop=n == len(parts) - 1)
                    mm.then_inc(ready(("S", L, h)), 1)
                if 1 <= h <= heads:
                    s = (h - 1) % 2
                    te.wait_ge(R["probs_normed"], h)
                    ps = open_job(te, ("PT", L, h - 1))
                    for b in range(3):
                        mm = nc.tensor.transpose(ps[:, b * P:(b + 1) * P], P_sb[:, s, b * P:(b + 1) * P], ident[:])
                    mm.then_inc(ready(("PT", L, h - 1)), 1)
                piece(te, h)
                if 1 <= h <= heads:
                    for key in v_waits(h - 1):
                        job_copied(te, key)
                    job_copied(te, ("PT", L, h - 1))
                    ps = open_job(te, ("O", L, h - 1))
                    nc.tensor.matmul(ps[:, 0:SEQ], v_of(h - 1, 0), PT_sb[:, s, 0:SEQ], start=True, stop=False)
                    nc.tensor.matmul(ps[:, P:SEQ], v_of(h - 1, 1), PT_sb[:, s, SEQ:3 * P], start=False,
                                     stop=True).then_inc(ready(("O", L, h - 1)), 1)
                if h >= 3 and h % 2 == 1:
                    p = (h - 3) // 2
                    job_copied(te, ("O", L, 2 * p))
                    job_copied(te, ("O", L, 2 * p + 1))
                    pe_out(te, ("wo", L, p), (ohi[:, p % 2], olo[:, p % 2]), p == 0, p == heads // 2 - 1)

        def act_attn(act, L, heads, piece):
            R = at_sems[L]
            for h in range(heads + 2):
                if h < heads:
                    s = h % 2
                    act.wait_ge(R["scores_masked"], h + 1)
                    nc.scalar.activation(P_sb[:, s, 0:P], S_sb[:, s, 0:P], ACT.Exp, bias=nmx[:, s, 0:1],
                                         accum_out=rsum[:, s, 0:1])
                    nc.scalar.activation(P_sb[:, s, P:3 * P], S_sb[:, s, P:3 * P], ACT.Exp, bias=nmx[:, s, 1:2],
                                         accum_out=rsum[:, s, 1:2]).then_inc(R["exp_done"], 1)
                if 1 <= h <= heads:
                    ps = job_ready(act, ("PT", L, h - 1))
                    nc.scalar.activation(PT_sb[:, (h - 1) % 2, :], ps[:, 0:3 * P],
                                         ACT.Copy).then_inc(freed(("PT", L, h - 1)), 1)
                piece(act, h)
                if 1 <= h <= heads:
                    hh = h - 1
                    p = hh // 2
                    ps = job_ready(act, ("O", L, hh))
                    if p >= 2:
                        act.wait_ge(*used(("wo", L, p - 2)))
                    nc.scalar.activation(ohi[:, p % 2, hh % 2, :], ps[:, 0:SEQ], ACT.Copy).then_inc(R["o_hi_done"], 1)
                if h >= 3 and h % 2 == 1:
                    act_splits(act, ("wo", L, (h - 3) // 2))

        def dve_attn(dve, L, heads, scale, mask_of, piece):
            R = at_sems[L]
            for h in range(heads + 2):
                if h < heads:
                    s = h % 2
                    ps = job_ready(dve, ("S", L, h))
                    nc.vector.scalar_tensor_tensor(out=S_sb[:, s, :], in0=ps[:, 0:3 * P], scalar=scale, in1=mask_of(h),
                                                   op0=ALU.mult, op1=ALU.add).then_inc(freed(("S", L, h)), 1)
                    job_copied(dve, ("S", L, h))
                    nc.vector.tensor_reduce(mx[:, s, 0:1], S_sb[:, s, 0:P], AX.X, ALU.max)
                    link(dve, nc.vector.tensor_reduce(mx[:, s, 1:2], S_sb[:, s, P:3 * P], AX.X, ALU.max))
                    nc.vector.tensor_scalar(nmx[:, s, :], mx[:, s, :], -1.0, None,
                                            ALU.mult).then_inc(R["scores_masked"], 1)
                piece(dve, h)
                if h < heads:
                    dve.wait_ge(R["exp_done"], h + 1)
                    link(dve, nc.vector.reciprocal(rinv[:, s, :], rsum[:, s, :]))
                    nc.vector.tensor_scalar(P_sb[:, s, 0:P], P_sb[:, s, 0:P], rinv[:, s, 0:1], None, ALU.mult)
                    nc.vector.tensor_scalar(P_sb[:, s, P:3 * P], P_sb[:, s, P:3 * P], rinv[:, s, 1:2], None,
                                            ALU.mult).then_inc(R["probs_normed"], 1)
                if 1 <= h <= heads:
                    hh = h - 1
                    p = hh // 2
                    dve.wait_ge(R["o_hi_done"], hh + 1)
                    nc.vector.tensor_tensor(olo[:, p % 2, hh % 2, :], bank[jobs.at["O", L, hh][0]][:, 0:SEQ],
                                            ohi[:, p % 2, hh % 2, :].bitcast(F32),
                                            ALU.subtract).then_inc(freed(("O", L, hh)), 1)
                if h >= 3 and h % 2 == 1:
                    dve_splits(dve, ("wo", L, (h - 3) // 2))

        def pe_mla_piece(te, L, g, q):
            s = g % 2
            HW, KW = NOPE + ROPE, NOPE + VD
            if q == 0:
                wait_unit(te, ("uq", L, g))
                wh, wl = (w.rearrange("p k (h d) -> p k h d", h=MLA_GRP) for w in hi_lo(("uq", L, g)))
                ps = open_job(te, ("qpe", L, g))
                for t in range(T):
                    dst = ps[:, t * 256:(t + 1) * 256].rearrange("p (h d) -> p h d", h=MLA_GRP)
                    for k in range(2):
                        mm = mm3(dst, (chi[:, k, tok(t)], clo[:, k, tok(t)]),
                                 (wh[:, k, :, NOPE:HW], wl[:, k, :, NOPE:HW]), k == 0, k == 1)
                mm.then_inc(ready(("qpe", L, g)), 1)
            if q == 1:
                wh, wl = hi_lo(("uq", L, g))
                for pr in range(2):
                    ps = open_job(te, ("qn", L, g, pr))
                    for hh in range(2):
                        n = slice(HW * (2 * pr + hh), HW * (2 * pr + hh) + NOPE)
                        for k in range(2):
                            mm = mm3(ps[:, hh * SEQ:(hh + 1) * SEQ], (wh[:, k, n], wl[:, k, n]),
                                     (chi[:, k, :], clo[:, k, :]), k == 0, k == 1)
                    mm.then_inc(ready(("qn", L, g, pr)), 1)
            if q == 2:
                te.wait_ge(mla_sems[L]["q_roped"], T * (g + 1))
                ps = open_job(te, ("qpT", L, g))
                for pr in range(2):
                    for t in range(T):
                        mm = nc.tensor.transpose(ps[:, pr * SEQ + t * P:pr * SEQ + (t + 1) * P],
                                                 qp[:, t, 2 * pr:2 * pr + 2, :].rearrange("p h d -> p (h d)"), ident[:])
                mm.then_inc(ready(("qpT", L, g)), 1)
                wait_unit(te, ("ukv", L, g))
                wh, wl = hi_lo(("ukv", L, g))
                for pr in range(2):
                    ps = open_job(te, ("kn", L, g, pr))
                    for hh in range(2):
                        n = slice(KW * (2 * pr + hh), KW * (2 * pr + hh) + NOPE)
                        for k in range(2):
                            mm = mm3(ps[:, hh * SEQ:(hh + 1) * SEQ], (wh[:, k, n], wl[:, k, n]),
                                     (chi[:, 2 + k, :], clo[:, 2 + k, :]), k == 0, k == 1)
                    mm.then_inc(ready(("kn", L, g, pr)), 1)
            if q == 3:
                wh, wl = (w.rearrange("p k (h d) -> p k h d", h=MLA_GRP) for w in hi_lo(("ukv", L, g)))
                for t in range(T):
                    ps = open_job(te, ("v", L, g, t))
                    dst = ps[:].rearrange("p (h d) -> p h d", h=MLA_GRP)
                    for k in range(2):
                        mm = mm3(dst, (chi[:, 2 + k, tok(t)], clo[:, 2 + k, tok(t)]),
                                 (wh[:, k, :, NOPE:KW], wl[:, k, :, NOPE:KW]), k == 0, k == 1)
                    mm.then_inc(ready(("v", L, g, t)), 1)

        def act_mla_piece(act, L, g, q):
            s = g % 2
            if q == 0:
                act_splits(act, ("uq", L, g))
            if q == 1:
                for pr in range(2):
                    ps = job_ready(act, ("qn", L, g, pr))
                    nc.scalar.activation(qT[:, s, 2 * pr:2 * pr + 2, :], ps[:].rearrange("p (h n) -> p h n", h=2),
                                         ACT.Copy).then_inc(freed(("qn", L, g, pr)), 1)
            if q == 2:
                act_splits(act, ("ukv", L, g))
            if q == 3:
                for t in range(T):
                    ps = job_ready(act, ("v", L, g, t))
                    nc.scalar.activation(v_sb[:, s, t, :], ps[:], ACT.Copy).then_inc(freed(("v", L, g, t)), 1)

        def dve_rope(dve, t, heads, src, src_freed, dst, done, dup):
            half = ROPE // 2
            c = csn[:, t, 0].rearrange("p a b -> p (a b)").unsqueeze(1).to_broadcast([P, heads, ROPE])
            nc.vector.tensor_tensor(ropa[:, t, 0:heads, :], src, c, ALU.mult)
            sn = [csn[:, t, 1, i, :].unsqueeze(1).to_broadcast([P, heads, half]) for i in range(2)]
            nc.vector.tensor_tensor(ropb[:, t, 0:heads, 0:half], src[:, :, half:ROPE], sn[0], ALU.mult)
            ins = nc.vector.tensor_tensor(ropb[:, t, 0:heads, half:ROPE], src[:, :, 0:half], sn[1], ALU.mult)
            if src_freed is None:
                link(dve, ins)
            else:
                ins.then_inc(src_freed[0], 1)
                dve.wait_ge(*src_freed)
            a, b = ropa[:, t, 0:heads, :], ropb[:, t, 0:heads, :]
            if dup:
                a, b = a.to_broadcast([P, 2, ROPE]), b.to_broadcast([P, 2, ROPE])
            nc.vector.tensor_tensor(dst, a, b, ALU.add).then_inc(done, 1)

        def dve_mla_piece(dve, L, g, q):
            s = g % 2
            if q == 0:
                dve_splits(dve, ("uq", L, g))
                ps = job_ready(dve, ("qpe", L, g))
                for t in range(T):
                    src = ps[:, t * 256:(t + 1) * 256].rearrange("p (h d) -> p h d", h=MLA_GRP)
                    dve_rope(dve, t, MLA_GRP, src, jobs.at["qpe", L, g][2] if t == T - 1 else None, qp[:, t],
                             mla_sems[L]["q_roped"], False)
            if q == 2:
                dve_splits(dve, ("ukv", L, g))
                ps = job_ready(dve, ("qpT", L, g))
                nc.vector.tensor_copy(qpT[:, s], ps[:].rearrange("p (h n) -> p h n", h=2)).then_inc(freed(("qpT", L, g)), 1)
                for pr in range(2):
                    ps = job_ready(dve, ("kn", L, g, pr))
                    nc.vector.tensor_copy(kT[:, s, 2 * pr:2 * pr + 2, :],
                                          ps[:].rearrange("p (h n) -> p h n", h=2)).then_inc(freed(("kn", L, g, pr)), 1)

        def pe_mla(te, j, L):
            M = mla_sems[L]
            banks = [open_job(te, ("c", L, t)) for t in range(T)]
            for n, name in enumerate(("cq", "ckv")):
                wait_unit(te, (name, L))
                w = hi_lo((name, L))
                for t in range(T):
                    for k in range(KD):
                        mm = mm3(banks[t][:, n * 256:(n + 1) * 256], (hhi[:, k, tok(t)], hlo[:, k, tok(t)]),
                                 (w[0][:, k, :], w[1][:, k, :]), k == 0, k == KD - 1)
                    if n == 1 and t == 0:
                        mm.then_inc(ready(("c", L, 0)), 1)
                mm.then_inc(used((name, L))[0], 1)
            wait_unit(te, ("kpe", L))
            w = hi_lo(("kpe", L))
            ps = open_job(te, ("kpe", L))
            for t in range(T):
                for k in range(KD):
                    mm = mm3(ps[:, t * ROPE:(t + 1) * ROPE], (hhi[:, k, tok(t)], hlo[:, k, tok(t)]),
                             (w[0][:, k, :], w[1][:, k, :]), k == 0, k == KD - 1)
            mm.then_inc(used(("kpe", L))[0], 1)
            for t in range(T):
                te.wait_ge(M["cn_done"], 2 * (t + 1))
                ps = open_job(te, ("ct", L, t))
                for b in range(4):
                    mm = nc.tensor.transpose(ps[:, b * P:(b + 1) * P], cn[:, t, b * P:(b + 1) * P], ident[:])
                mm.then_inc(ready(("ct", L, t)), 1)
            te.wait_ge(M["kp_done"], T)
            ps = open_job(te, ("kpT", L))
            for t in range(T):
                mm = nc.tensor.transpose(ps[:, tok(t)], kp[:, t].rearrange("p a d -> p (a d)"), ident[:])
            mm.then_inc(ready(("kpT", L)), 1)
            for t in range(T):
                job_copied(te, ("ct", L, t))
            for q in range(4):
                pe_mla_piece(te, L, 0, q)

            def qk(h):
                s, hh = (h // 4) % 2, h % 4
                r = slice(ROPE * (hh % 2), ROPE * (hh % 2) + ROPE)
                return [(qT[:, s, hh, :], kT[:, s, hh, :]), (qpT[r, s, hh // 2, :], kpT[r, :])]

            def qk_waits(h):
                g, hh = h // 4, h % 4
                return [("qn", L, g, hh // 2), ("kn", L, g, hh // 2), ("qpT", L, g), ("kpT", L)] if hh % 2 == 0 else []

            pe_attn(te, L, MLA_H, qk, qk_waits,
                    lambda h, t: v_sb[:, (h // 4) % 2, t, (h % 4) * VD:(h % 4 + 1) * VD],
                    lambda h: [("v", L, h // 4, 0), ("v", L, h // 4, 1)] if h % 4 == 0 else [],
                    lambda te, h: pe_mla_piece(te, L, h // 4 + 1, h % 4) if h < MLA_H - MLA_GRP else None)

        def act_mla(act, j, L, i):
            M = mla_sems[L]
            act_splits(act, ("cq", L))
            act_splits(act, ("ckv", L))
            for t in range(T):
                ps = job_ready(act, ("c", L, t))
                for n in range(2):
                    if t or n:
                        act.wait_ge(M["c_ssq_done"], 2 * t + n)
                    nc.scalar.activation(junk[:, 0:256], ps[:, 256 * n:256 * (n + 1)], ACT.Square,
                                         accum_out=c_ssq[:, i, t, n:n + 1]).then_inc(M["c_ssq_done"], 1)
            act_splits(act, ("kpe", L))
            for t in range(T):
                ps = job_ready(act, ("ct", L, t))
                nc.scalar.activation(chi[:, :, tok(t)], ps[:].rearrange("p (b n) -> p b n", b=4),
                                     ACT.Copy).then_inc(M["c_hi_done"], 1)
            ps = job_ready(act, ("kpT", L))
            nc.scalar.activation(kpT[:], ps[:, 0:SEQ], ACT.Copy).then_inc(freed(("kpT", L)), 1)
            for q in range(4):
                act_mla_piece(act, L, 0, q)
            act_attn(act, L, MLA_H, lambda act, h: act_mla_piece(act, L, h // 4 + 1, h % 4)
                     if h < MLA_H - MLA_GRP else None)

        def dve_mla(dve, j, L, i):
            M = mla_sems[L]
            dve_splits(dve, ("cq", L))
            dve_splits(dve, ("ckv", L))
            for t in range(T):
                dve.wait_ge(M["c_ssq_done"], 2 * (t + 1))
                nc.vector.tensor_scalar(c_ms[:, i, t, :], c_ssq[:, i, t, :], 1.0 / QR, EPS, ALU.mult,
                                        ALU.add).then_inc(M["c_ms_done"], 1)
            dve.wait_ge(qkvg_loaded, 64)
            for t in range(T):
                dve.wait_ge(M["c_rstd_done"], t + 1)
                for n in range(2):
                    c = slice(256 * n, 256 * (n + 1))
                    nc.vector.scalar_tensor_tensor(out=cn[:, t, c], in0=bank[jobs.at["c", L, t][0]][:, c],
                                                   scalar=c_rstd[:, i, t, n:n + 1], in1=qkvg[:, i, c], op0=ALU.mult,
                                                   op1=ALU.mult).then_inc(M["cn_done"], 1)
            dve.wait_ge(sin_done, 3)
            ps = job_ready(dve, ("kpe", L))
            for t in range(T):
                src = ps[:, t * ROPE:(t + 1) * ROPE].unsqueeze(1)
                dve_rope(dve, t, 1, src, jobs.at["kpe", L][2] if t == T - 1 else None, kp[:, t], M["kp_done"], True)
            for t in range(T):
                dve.wait_ge(M["c_hi_done"], t + 1)
                nc.vector.tensor_tensor(clo[:, :, tok(t)], bank[jobs.at["ct", L, t][0]][:].rearrange("p (b n) -> p b n", b=4),
                                        chi[:, :, tok(t)].bitcast(F32), ALU.subtract).then_inc(freed(("ct", L, t)), 1)
            dve_splits(dve, ("kpe", L))
            for q in range(4):
                dve_mla_piece(dve, L, 0, q)
            dve_attn(dve, L, MLA_H, MLA_SCALE, lambda h: mask[:],
                     lambda dve, h: dve_mla_piece(dve, L, h // 4 + 1, h % 4) if h < MLA_H - MLA_GRP else None)

        def pool_mla(pool, L, i):
            M = mla_sems[L]
            for t in range(T):
                pool.wait_ge(M["c_ms_done"], t + 1)
                nc.gpsimd.tensor_tensor(c_rstd[:, i, t, :], c_ms[:, i, t, :], neghalf[:, 0:2],
                                        ALU.pow).then_inc(M["c_rstd_done"], 1)

        def pe_moba_piece(te, L, h):
            if h % 2 == 0:
                key = ("mv", L, h // 2)
                wait_unit(te, key)
                w = hi_lo(key)
                ps = open_job(te, key)
                for t in range(T):
                    for k in range(KD):
                        mm = mm3(ps[:, t * 256:(t + 1) * 256], (hhi[:, k, tok(t)], hlo[:, k, tok(t)]),
                                 (w[0][:, k, :], w[1][:, k, :]), k == 0, k == KD - 1)
                mm.then_inc(used(key)[0], 1)
            key = ("mqk", L, h)
            wait_unit(te, key)
            w = hi_lo(key)
            ps = open_job(te, key)
            for n in range(2):
                for k in range(KD):
                    mm = mm3(ps[:, n * SEQ:(n + 1) * SEQ], (w[0][:, k, tok(n)], w[1][:, k, tok(n)]),
                             (hhi[:, k, :], hlo[:, k, :]), k == 0, k == KD - 1)
            mm.then_inc(used(key)[0], 1)

        def act_moba_piece(act, L, h):
            if h % 2 == 0:
                key = ("mv", L, h // 2)
                act_splits(act, key)
                ps = job_ready(act, key)
                nc.scalar.activation(v_sb[:, (h // 2) % 2, :, 0:256], ps[:].rearrange("p (t n) -> p t n", t=T),
                                     ACT.Copy).then_inc(freed(key), 1)
            key = ("mqk", L, h)
            act_splits(act, key)
            ps = job_ready(act, key)
            nc.scalar.activation(qT[:, h % 2, 0, :], ps[:, 0:SEQ], ACT.Copy)
            nc.scalar.activation(kT[:, h % 2, 0, :], ps[:, SEQ:2 * SEQ], ACT.Copy).then_inc(freed(key), 1)

        def dve_moba_piece(dve, L, h):
            if h % 2 == 0:
                dve_splits(dve, ("mv", L, h // 2))
            dve_splits(dve, ("mqk", L, h))

        def pe_moba(te, j, L):
            pe_moba_piece(te, L, 0)
            pe_attn(te, L, MOBA_H, lambda h: [(qT[:, h % 2, 0, :], kT[:, h % 2, 0, :])],
                    lambda h: [("mqk", L, h)],
                    lambda h, t: v_sb[:, (h // 2) % 2, t, (h % 2) * P:(h % 2 + 1) * P],
                    lambda h: [("mv", L, h // 2)],
                    lambda te, h: pe_moba_piece(te, L, h + 1) if h < MOBA_H - 1 else None)

        def act_moba(act, j, L):
            act_moba_piece(act, L, 0)
            act_attn(act, L, MOBA_H, lambda act, h: act_moba_piece(act, L, h + 1) if h < MOBA_H - 1 else None)

        def dve_moba(dve, j, L):
            dve_moba_piece(dve, L, 0)
            dve.wait_ge(bias_loaded, 32)
            dve_attn(dve, L, MOBA_H, MOBA_SCALE, lambda h: bias[:, h, :],
                     lambda dve, h: dve_moba_piece(dve, L, h + 1) if h < MOBA_H - 1 else None)

        def pe_bias(te):
            te.wait_ge(rel_loaded, 32)
            te.wait_ge(pool_const, 2)
            ps = open_job(te, "bias")
            nc.tensor.matmul(ps[0:MOBA_H, 0:384], relx[:], onehot[:], start=True, stop=True).then_inc(ready("bias"), 1)

        def dve_bias(dve):
            ps = job_ready(dve, "bias")
            nc.vector.tensor_copy(biasrow[:], ps[0:MOBA_H, 0:384]).then_inc(freed("bias"), 1)

        def pool_bias_store(pool):
            job_copied(pool, "bias")
            pool.dma_start(bias_dram, biasrow[:].unsqueeze(1).to_broadcast([MOBA_H, P, 384])).then_inc(brow_stored, 16)

        def pool_bias_load(pool, j):
            pool.wait_ge(brow_stored, 16)
            wait_x(pool, j, T - 1)
            for dst, off, n in ((bias[:, :, P:3 * P], P - 1, 2 * P), (bias[:, :, 0:P], 2 * P - 1, P)):
                src = bass.AP(bias_dram.tensor, off, [[383, P], [P * 384, MOBA_H], [1, n]])
                pool.dma_start(dst, src).then_inc(bias_loaded, 16)

        DT, EXP, U, LN, DD, DEC, DTO, ACS = range(8)

        def pe_ssd(te, j, L):
            h = (hhi, hlo)
            wait_unit(te, "dt")
            w = hi_lo("dt")
            ps = open_job(te, "dt")
            for k in range(KD):
                mm = mm3(ps[0:SSD_H, 0:SEQ], (w[0][:, k, :], w[1][:, k, :]), (hhi[:, k, :], hlo[:, k, :]), k == 0,
                         k == KD - 1)
            mm.then_inc(used("dt")[0], 1)
            te.wait_ge(ssd_loaded, 96)
            te.wait_ge(drows_done, 1)
            ps = open_job(te, "scol")
            nc.tensor.transpose(ps[:, 0:116], crows[0:116, :], ident[0:116, 0:116])
            nc.tensor.transpose(ps[:, P:P + ZT], drows[:].rearrange("p a b -> p (a b)"),
                                ident[0:ZT, 0:ZT]).then_inc(ready("scol"), 1)

            def proj(key):
                wait_unit(te, key)
                w = hi_lo(key)
                ps = open_job(te, key)
                for m in range(2):
                    for k in range(KD):
                        mm = mm3(ps[:, m * SEQ:(m + 1) * SEQ], (w[0][:, k, tok(m)], w[1][:, k, tok(m)]),
                                 (hhi[:, k, :], hlo[:, k, :]), k == 0, k == KD - 1)
                mm.then_inc(used(key)[0], 1)

            for n in range(10):
                proj(("cv", n))
                if n == 4:
                    te.wait_ge(dt_out, 1)
                    te.wait_ge(acs_done, 1)
                    te.wait_ge(dec_io, 2)
                    ps = open_job(te, "tokv")
                    for i, (row, c) in enumerate(((DTO, 0), (DTO, 1), (ACS, 0), (ACS, 1), (DEC, 0), (DEC, 1))):
                        mm = nc.tensor.transpose(ps[:, i * SSD_H:(i + 1) * SSD_H], dtv[0:SSD_H, row, tok(c)],
                                                 ident[0:SSD_H, 0:SSD_H])
                    mm.then_inc(ready("tokv"), 1)
                    te.wait_ge(silu_done, 2)
                    ps = open_job(te, "cb")
                    for g in range(SSD_G):
                        for c in range(T):
                            i = g * T + c
                            mm = nc.tensor.matmul(ps[:, i * P:(i + 1) * P], BT[:, g, tok(c)], CT[:, g, tok(c)],
                                                  start=True, stop=True)
                    mm.then_inc(ready("cb"), 1)
                    ps = open_job(te, "Btok")
                    for g in range(SSD_G):
                        mm = nc.tensor.transpose(ps[:, g * P:(g + 1) * P], BT[:, g, tok(0)], ident[:])
                    mm.then_inc(ready("Btok"), 1)
            job_copied(te, "Btok")
            for q in range(5):
                g = q // 2
                if q < 4:
                    te.wait_ge(silu_done, 2 + 2 * q + 2)
                    for c in range(T):
                        ps = open_job(te, ("xT", q, c))
                        for i in range(4):
                            mm = nc.tensor.transpose(ps[:, i * P:(i + 1) * P], xsT[:, 4 * q + i, tok(c)], ident[:])
                        mm.then_inc(ready(("xT", q, c)), 1)
                    proj(("z", 2 * q))
                    te.wait_ge(dx_done, q + 1)
                    ps = open_job(te, ("st", q))
                    nc.tensor.matmul(ps[:], Btok[:, g, :], dxdt, start=True, stop=True).then_inc(ready(("st", q)), 1)
                    proj(("z", 2 * q + 1))
                    job_copied(te, ("st", q))

                    def ydiag(c):
                        te.wait_ge(dec_ready, 2 * q + c + 1)
                        job_copied(te, ("xT", q, c))
                        ps = open_job(te, ("yd", q, c))
                        for hh in range(8):
                            mm = nc.tensor.matmul(ps[:, hh * SSD_HD:(hh + 1) * SSD_HD], dec[:, (2 * q + c) % 4, hh, :],
                                                  xdt[:, c, hh * SSD_HD:(hh + 1) * SSD_HD], start=True, stop=True)
                        mm.then_inc(ready(("yd", q, c)), 1)

                    ydiag(0)
                    ps = open_job(te, ("yo", q))
                    nc.tensor.matmul(ps[:], CT[:, g, tok(1)], prevT, start=True, stop=True).then_inc(ready(("yo", q)), 1)
                    ydiag(1)

                def sums(g):
                    te.wait_ge(gadd_done, 4 * (g + 1))
                    ps = open_job(te, ("ss", g))
                    for t in range(T):
                        for i in range(2):
                            mm = nc.tensor.matmul(ps[:, t:t + 1], gss[:, i * SEQ + t * P:i * SEQ + (t + 1) * P],
                                                  ones[:, 0:1], start=i == 0, stop=i == 1)
                    mm.then_inc(ready(("ss", g)), 1)

                if q == 2:
                    sums(0)
                for n in (2 * q - 2, 2 * q - 1) if q else ():
                    te.wait_ge(glo_done, n + 1)
                    if n == 4:
                        te.wait_ge(ssd_half, 2 * T)
                    if n == 7:
                        sums(1)
                    pe_out(te, ("so", L, n), (ghi[:, n % 2], glo[:, n % 2]), n % 4 == 0, n % 4 == 3)
                if q < 4:
                    job_copied(te, ("yd", q, 0))
                    job_copied(te, ("yd", q, 1))
                    for u in range(2):
                        ps = open_job(te, ("yT", q, u))
                        for i in range(2):
                            for c in range(T):
                                mm = nc.tensor.transpose(ps[:, i * SEQ + c * P:i * SEQ + (c + 1) * P],
                                                         y_sb[:, c, (2 * u + i) * P:(2 * u + i + 1) * P], ident[:])
                        mm.then_inc(ready(("yT", q, u)), 1)

        def act_ssd(act, j, L):
            v = dtv[0:SSD_H]
            act_splits(act, "dt")
            act.wait_ge(ssd_loaded, 96)
            nc.scalar.activation(headc[:, 2:3], headc[:, 1:2], ACT.Exp).then_inc(da_done, 1)
            act.wait_ge(dt_abs, 1)
            nc.scalar.activation(v[:, EXP, :], v[:, U, :], ACT.Exp, scale=-1.0).then_inc(dt_exp, 1)
            act.wait_ge(dt_u, 1)
            nc.scalar.activation(v[:, LN, :], v[:, U, :], ACT.Ln).then_inc(dt_ln, 1)
            ps = job_ready(act, "scol")
            nc.scalar.activation(scol[:, 0:116], ps[:, 0:116], ACT.Copy)
            nc.scalar.activation(scol[:, P:P + ZT], ps[:, P:P + ZT], ACT.Copy).then_inc(freed("scol"), 1)
            job_copied(act, "scol")
            dst = [BT, CT] + [xsT[:, 2 * n:2 * n + 2, :] for n in range(ZT // 2)]

            def silu(n):
                act.wait_ge(conv_done, n + 1)
                nc.scalar.activation(dst[n][:] if n < 2 else dst[n], cacc[:, n % 2], ACT.Silu).then_inc(silu_done, 1)

            for n in range(10):
                act_splits(act, ("cv", n))
                ps = job_ready(act, ("cv", n))
                s = n % 2
                if n >= 2:
                    act.wait_ge(silu_done, n - 1)
                nc.scalar.activation(cvin[:, s, :, SSD_CONV - 1:], ps[:].rearrange("p (i n) -> p i n", i=2), ACT.Copy)
                for i in range(2):
                    tile = 16 + 2 * n + i if n < 2 else 2 * (n - 2) + i
                    ins = nc.scalar.activation(cacc[:, s, i, :], ps[:, i * SEQ:(i + 1) * SEQ], ACT.Identity,
                                               bias=scol[:, 80 + tile:81 + tile], scale=scol[:, 60 + tile:61 + tile])
                ins.then_inc(freed(("cv", n)), 1)
                if n == 1:
                    act.wait_ge(acs_done, 1)
                    for i in range(2):
                        ins = nc.scalar.activation(v[:, DEC, tok(i)], v[:, ACS, tok(i)], ACT.Exp,
                                                   bias=v[:, ACS, P - 1:P] if i == 0 else 0.0,
                                                   scale=-1.0 if i == 0 else 1.0).then_inc(dec_io, 1)
                if n:
                    silu(n - 1)
                if n == 4:
                    ps = job_ready(act, "Btok")
                    nc.scalar.activation(Btok[:].rearrange("p a b -> p (a b)"), ps[:, 0:SSD_G * P],
                                         ACT.Copy).then_inc(freed("Btok"), 1)
            silu(9)
            act.wait_ge(silu_done, 10)

            def decays(q):
                for c in range(T):
                    b = (2 * q + c) % 4
                    act.wait_ge(dec_diff, 2 * q + c + 1)
                    nc.scalar.activation(dec[:, b], dec[:, b], ACT.Exp).then_inc(dec_exp, 1)

            decays(0)
            for q in range(5):
                if q < 4:
                    for u in range(2):
                        n = 2 * q + u
                        act_splits(act, ("z", n))
                        ps = job_ready(act, ("z", n))
                        nc.scalar.activation(sz[:, n % 2].rearrange("p a b -> p (a b)"), ps[:],
                                             ACT.Silu).then_inc(freed(("z", n)), 1)
                        if u == 0:
                            ps = job_ready(act, ("st", q))
                            nc.scalar.activation(prevT, ps[:], ACT.Copy).then_inc(freed(("st", q)), 1)
                    ps = job_ready(act, ("yd", q, 0))
                    nc.scalar.activation(y_sb[:, 0, :], ps[:], ACT.Copy).then_inc(freed(("yd", q, 0)), 1)
                if q < 3:
                    decays(q + 1)
                if q:
                    act_splits(act, ("so", L, 2 * q - 2))
                    act_splits(act, ("so", L, 2 * q - 1))
                if q < 4:
                    for u in range(2):
                        n = 2 * q + u
                        act.wait_ge(g_done, n + 1)
                        if n:
                            act.wait_ge(gadd_done, n)
                        nc.scalar.activation(gsq[:], gy[:, n % 2].rearrange("p a b -> p (a b)"),
                                             ACT.Square).then_inc(gsq_done, 1)
                        if n >= 2:
                            act.wait_ge(*used(("so", L, n - 2)))
                        for i in range(2):
                            ins = nc.scalar.activation(ghi[:, n % 2, i, :], gy[:, n % 2, i, :], ACT.Copy,
                                                       scale=scol[:, 100 + 2 * n + i:101 + 2 * n + i])
                        ins.then_inc(ghi_done, 1)

        def dve_ssd(dve, j, L):
            v = dtv[0:SSD_H]
            dve.wait_ge(ssd_loaded, 96)
            nc.vector.tensor_copy(drows[:], drow[:].unsqueeze(2).to_broadcast([ZT, 2, SSD_HD])).then_inc(drows_done, 1)
            nc.vector.memset(cvin[:, :, :, 0:SSD_CONV - 1], 0.0)
            dve_splits(dve, "dt")
            ps = job_ready(dve, "dt")
            nc.vector.tensor_scalar(v[:, DT, :], ps[0:SSD_H, 0:SEQ], headc[:, 0:1], None, ALU.add).then_inc(freed("dt"), 1)
            job_copied(dve, "dt")
            nc.vector.scalar_tensor_tensor(out=v[:, U, :], in0=v[:, DT, :], scalar=-1.0, in1=v[:, DT, :], op0=ALU.mult,
                                           op1=ALU.max).then_inc(dt_abs, 1)
            dve.wait_ge(dt_exp, 1)
            nc.vector.tensor_scalar(v[:, U, :], v[:, EXP, :], 1.0, None, ALU.add).then_inc(dt_u, 1)
            dve.wait_ge(dt_u, 1)
            link(dve, nc.vector.tensor_scalar(v[:, DD, :], v[:, U, :], 1.0, None, ALU.subtract))
            link(dve, nc.vector.tensor_scalar(v[:, DEC, :], v[:, DD, :], 0.0, None, ALU.is_equal))
            link(dve, nc.vector.tensor_tensor(v[:, DD, :], v[:, DD, :], v[:, DEC, :], ALU.add))
            link(dve, nc.vector.reciprocal(v[:, DD, :], v[:, DD, :]))
            dve.wait_ge(dt_ln, 1)
            link(dve, nc.vector.tensor_tensor(v[:, LN, :], v[:, LN, :], v[:, DEC, :], ALU.add))
            link(dve, nc.vector.tensor_tensor(v[:, LN, :], v[:, LN, :], v[:, DD, :], ALU.mult))
            link(dve, nc.vector.tensor_tensor(v[:, LN, :], v[:, LN, :], v[:, EXP, :], ALU.mult))
            nc.vector.scalar_tensor_tensor(out=v[:, DTO, :], in0=v[:, DT, :], scalar=0.0, in1=v[:, LN, :], op0=ALU.max,
                                           op1=ALU.add).then_inc(dt_out, 1)
            dve.wait_ge(dt_out, 1)
            dve.wait_ge(da_done, 1)
            link(dve, nc.vector.tensor_scalar(v[:, DD, :], v[:, DTO, :], headc[:, 2:3], -1.0, ALU.mult, ALU.mult))
            for c in range(T):
                ins = nc.vector.tensor_tensor_scan(v[:, ACS, tok(c)], ones[0:SSD_H, :].to_broadcast([SSD_H, P]), v[:, DD, tok(c)], 0.0, ALU.mult,
                                                   ALU.add)
            ins.then_inc(acs_done, 1)

            def conv(n):
                dve_splits(dve, ("cv", n))
                job_copied(dve, ("cv", n))
                s = n % 2
                for tap in range(SSD_CONV - 2, -1, -1):
                    for i in range(2):
                        tile = 16 + 2 * n + i if n < 2 else 2 * (n - 2) + i
                        ins = nc.vector.scalar_tensor_tensor(out=cacc[:, s, i, :], in0=cvin[:, s, i, tap:tap + SEQ],
                                                             scalar=scol[:, 20 * tap + tile:20 * tap + tile + 1],
                                                             in1=cacc[:, s, i, :], op0=ALU.mult, op1=ALU.add)
                    if tap:
                        link(dve, ins)
                ins.then_inc(conv_done, 1)

            def diffs(q):
                for c in range(T):
                    b = (2 * q + c) % 4
                    dve.wait_ge(dec_loaded[b], 16 * (q // 2 + 1))
                    for hh in range(8):
                        ins = nc.vector.tensor_scalar(dec[:, b, hh, :], dec[:, b, hh, :],
                                                      tokv[:, 2 + c, 8 * q + hh:8 * q + hh + 1], 0.0, ALU.subtract,
                                                      ALU.min)
                    ins.then_inc(dec_diff, 1)

            def decay_cb(q, c):
                b = (2 * q + c) % 4
                dve.wait_ge(dec_exp, 2 * q + c + 1)
                nc.vector.tensor_tensor(dec[:, b], dec[:, b], cbm[:, q // 2, c, :].unsqueeze(1).to_broadcast([P, 8, P]),
                                        ALU.mult).then_inc(dec_ready, 1)

            for n in range(10):
                conv(n)
                if n == 4:
                    ps = job_ready(dve, "tokv")
                    nc.vector.tensor_copy(tokv[:].rearrange("p a b -> p (a b)"),
                                          ps[:, 0:6 * SSD_H]).then_inc(freed("tokv"), 1)
                    job_copied(dve, "tokv")
                    dve.wait_ge(upper_loaded, 16)
                    ps = job_ready(dve, "cb")
                    nc.vector.tensor_tensor(cbm[:].rearrange("p g c l -> p (g c) l"), ps[:].rearrange("p (a l) -> p a l", a=4),
                                            upper[:].unsqueeze(1).to_broadcast([P, 4, P]), ALU.mult).then_inc(freed("cb"), 1)
                if n == 8:
                    diffs(0)
            job_copied(dve, "cb")
            for c in range(T):
                decay_cb(0, c)
            for q in range(5):
                if q < 4:
                    hs = slice(8 * q, 8 * q + 8)
                    dve_splits(dve, ("z", 2 * q))
                    if q:
                        dve.wait_ge(dx_done, q)
                    for c in range(T):
                        ps = job_ready(dve, ("xT", q, c))
                        nc.vector.tensor_tensor(xdt[:, c, :].rearrange("p (h d) -> p h d", h=8),
                                                ps[:].rearrange("p (h d) -> p h d", h=8),
                                                tokv[:, c, hs].unsqueeze(2).to_broadcast([P, 8, SSD_HD]),
                                                ALU.mult).then_inc(freed(("xT", q, c)), 1)
                    job_copied(dve, ("xT", q, 0))
                    nc.vector.tensor_tensor(dxdt.rearrange("p (h d) -> p h d", h=8),
                                            xdt[:, 0, :].rearrange("p (h d) -> p h d", h=8),
                                            tokv[:, 4, hs].unsqueeze(2).to_broadcast([P, 8, SSD_HD]),
                                            ALU.mult).then_inc(dx_done, 1)
                    dve_splits(dve, ("z", 2 * q + 1))
                    if q < 3:
                        diffs(q + 1)
                    ps = job_ready(dve, ("yo", q))
                    nc.vector.tensor_tensor(y_sb[:, 1, :].rearrange("p (h d) -> p h d", h=8),
                                            ps[:].rearrange("p (h d) -> p h d", h=8),
                                            tokv[:, 5, hs].unsqueeze(2).to_broadcast([P, 8, SSD_HD]),
                                            ALU.mult).then_inc(freed(("yo", q)), 1)
                    job_copied(dve, ("yo", q))
                    ps = job_ready(dve, ("yd", q, 1))
                    nc.vector.tensor_tensor(y_sb[:, 1, :], ps[:], y_sb[:, 1, :], ALU.add).then_inc(freed(("yd", q, 1)), 1)
                if q in (2, 4):
                    g = q // 2 - 1

                    def mean_square():
                        ps = job_ready(dve, ("ss", g))
                        nc.vector.tensor_scalar(g_ms[:, g, :], ps[:, 0:T], SSD_G / SSD_IN, EPS, ALU.mult,
                                                ALU.add).then_inc(freed(("ss", g)), 1)

                    if g == 0:
                        mean_square()
                for n in (2 * q - 2, 2 * q - 1) if q else ():
                    dve_splits(dve, ("so", L, n))
                if q == 4:
                    mean_square()
                    dve.wait_ge(grstd_done, 2)
                if q < 4:
                    for u in range(2):
                        n = 2 * q + u
                        ps = job_ready(dve, ("yT", q, u))
                        if n >= 2:
                            dve.wait_ge(glo_done, n - 1)
                        for i in range(2):
                            tile = 2 * n + i
                            ins = nc.vector.scalar_tensor_tensor(out=gy[:, n % 2, i, :], in0=xsT[:, tile, :],
                                                                 scalar=scol[:, P + tile:P + tile + 1],
                                                                 in1=ps[:, i * SEQ:(i + 1) * SEQ], op0=ALU.mult,
                                                                 op1=ALU.add)
                        ins.then_inc(freed(("yT", q, u)), 1)
                        job_copied(dve, ("yT", q, u))
                        job_copied(dve, ("z", n))
                        nc.vector.tensor_tensor(gy[:, n % 2], gy[:, n % 2], sz[:, n % 2], ALU.mult).then_inc(g_done, 1)
                        if q < 3:
                            decay_cb(q + 1, u)
                        dve.wait_ge(ghi_done, n + 1)
                        for i in range(2):
                            ins = nc.vector.scalar_tensor_tensor(out=glo[:, n % 2, i, :], in0=gy[:, n % 2, i, :],
                                                                 scalar=scol[:, 100 + 2 * n + i:101 + 2 * n + i],
                                                                 in1=ghi[:, n % 2, i, :].bitcast(F32), op0=ALU.mult,
                                                                 op1=ALU.subtract)
                        ins.then_inc(glo_done, 1)
                if q == 2:
                    dve.wait_ge(grstd_done, 1)
                    for t in range(T):
                        if t == 0:
                            dve.wait_ge(acc_done, acc_rounds[j] - 1)
                        else:
                            dve.wait_ge(*used(("so", L, 3)))
                        for half in range(2):
                            c = slice(512 * half, 512 * half + 512)
                            nc.vector.scalar_tensor_tensor(out=x[:, t, c], in0=acc[t][half][:],
                                                           scalar=g_rstd[:, 0, t:t + 1], in1=x[:, t, c], op0=ALU.mult,
                                                           op1=ALU.add).then_inc(ssd_half, 1)
            dve.wait_ge(ssd_half, 2 * T)

        def pool_ssd(pool, j, L):
            def load(q):
                for c in range(T):
                    b = (2 * q + c) % 4
                    if q >= 2:
                        pool.wait_ge(*jobs.at["yd", q - 2, c][1])
                    src = acs_dram[8 * q:8 * q + 8, tok(c)].unsqueeze(0).to_broadcast([P, 8, P])
                    pool.dma_start(dec[:, b], src).then_inc(dec_loaded[b], 16)

            pool.wait_ge(acs_done, 1)
            pool.dma_start(acs_dram, dtv[0:SSD_H, ACS, :]).then_inc(acs_stored, 16)
            pool.wait_ge(acs_stored, 16)
            load(0)
            load(1)
            for n in range(8):
                g = n // 4
                pool.wait_ge(gsq_done, n + 1)
                if n % 4:
                    pool.wait_ge(gadd_done, n)
                    nc.gpsimd.tensor_tensor(gss[:], gss[:], gsq[:], ALU.add).then_inc(gadd_done, 1)
                else:
                    if g:
                        pool.wait_ge(*jobs.at["ss", 0][1])
                    nc.gpsimd.tensor_copy(gss[:], gsq[:]).then_inc(gadd_done, 1)
                if n in (1, 3):
                    load(n // 2 + 2)
                if n == 7 or n == 3:
                    pool.wait_ge(*jobs.at["ss", g][2])
                    pool.wait_ge(gadd_done, n + 1)
                    nc.gpsimd.tensor_tensor(g_rstd[:, g, :], g_ms[:, g, :], neghalf[:, 0:T], ALU.pow).then_inc(grstd_done, 1)

        def dve_angles(dve):
            dve.wait_ge(rope_loaded, 32)
            link(dve, nc.vector.tensor_copy(pos_f[:], pos_i[:]))
            for t in range(T):
                ins = nc.vector.tensor_scalar(ang[:, 0, t, :], invf[:], pos_f[:, t:t + 1], None, ALU.mult)
            link(dve, ins)
            a, k, r, w = (ang[:, n] for n in range(4))
            link(dve, nc.vector.tensor_scalar(k, a, 1.0 / (2 * math.pi), ROUND_MAGIC, ALU.mult, ALU.add))
            link(dve, nc.vector.tensor_scalar(k, k, ROUND_MAGIC, None, ALU.subtract))
            for n, c in enumerate((TWO_PI_A, TWO_PI_B, TWO_PI_C)):
                link(dve, nc.vector.scalar_tensor_tensor(out=r, in0=k, scalar=-c, in1=a if n == 0 else r, op0=ALU.mult,
                                                         op1=ALU.add))
            link(dve, nc.vector.tensor_scalar(a, r, math.pi / 2, None, ALU.add))
            link(dve, nc.vector.tensor_scalar(w, a, math.pi, -2 * math.pi, ALU.is_gt, ALU.mult))
            link(dve, nc.vector.tensor_tensor(a, a, w, ALU.add))
            nc.vector.tensor_scalar(r, r, PI_IN, -PI_IN, ALU.min, ALU.max)
            nc.vector.tensor_scalar(a, a, PI_IN, -PI_IN, ALU.min, ALU.max).then_inc(ang_done, 1)

        def act_angles(act):
            act.wait_ge(ang_done, 1)
            nc.scalar.activation(csn[:, :, 1, 0, :], ang[:, 2], ACT.Sin, scale=-1.0).then_inc(sin_done, 1)
            nc.scalar.activation(csn[:, :, 1, 1, :], ang[:, 2], ACT.Sin)
            for n in range(2):
                nc.scalar.activation(csn[:, :, 0, n, :], ang[:, 0], ACT.Sin).then_inc(sin_done, 1)

        block = ctx.enter_context(nc.Block())

        @block.sync
        def _(sp):
            sp.dma_start(x[:], A["x"][0].rearrange("(t p) d -> p t d", p=P)).then_inc(x_loaded, 16)
            sp.dma_start(ident[:], A["c_ident"]).then_inc(consts, 16)
            sp.dma_start(mask[:], A["c_mask"]).then_inc(consts, 16)

            def gains(j):
                if j >= NN:
                    return
                if j:
                    sp.wait_ge(xn_done, j * T)
                if j == NN - 1:
                    src = A["norm_final"].unsqueeze(0)
                else:
                    kind, L, _ = stages[j]
                    src = A["norm_mlp" if kind == "mlp" else "norm_mix"][L:L + 1, :]
                sp.dma_start(gbc[:], src.to_broadcast([P, DM])).then_inc(gain_loaded, 16)

            gains(0)
            for n, (a, b, srcs) in enumerate(units):
                s, k = n % SLOTS, n // SLOTS
                if n in stage_unit:
                    gains(stage_unit[n] + 1)
                if k:
                    sp.wait_ge(w_split[s], k)
                w = b // len(srcs)
                for i, src in enumerate(srcs):
                    dst = raw[:, s, :a * b].rearrange("p (a b) -> p a b", a=a)[:, :, i * w:(i + 1) * w]
                    sp.dma_start(dst, src).then_inc(raw_loaded[s], 16)
            for t in range(T):
                sp.wait_ge(xn_done, (NN - 1) * T + t + 1)
                sp.dma_start(out[0, t * P:(t + 1) * P, :], xn[:, t, :]).then_inc(out_stored, 16)
            sp.wait_ge(out_stored, 16 * T)

        @block.gpsimd
        def _(pool):
            nc.gpsimd.memset(neghalf[:], -0.5).then_inc(pool_const, 1)
            pool.wait_ge(pool_const, 1)
            nc.gpsimd.memset(relx[BUCKETS:BUCKETS + 1, :], 1.0).then_inc(pool_const, 1)
            pool.wait_ge(pool_const, 2)
            nc.gpsimd.memset(ones[:], 1.0).then_inc(pool_const, 1)
            pool.wait_ge(pool_const, 3)
            pool.dma_start(pos_i[:], A["positions"].rearrange("o (t p) -> p (o t)", p=P),
                           allow_slow_non_contiguous=True).then_inc(rope_loaded, 16)
            pool.dma_start(invf[:], A["c_invfreq"].to_broadcast([P, ROPE // 2])).then_inc(rope_loaded, 16)
            for i in range(2):
                pool.dma_start(qkvg[:, i, 0:QR], A["mla_q_norm"][i:i + 1, :].to_broadcast([P, QR])).then_inc(qkvg_loaded, 16)
                pool.dma_start(qkvg[:, i, QR:QR + KVR],
                               A["mla_kv_norm"][i:i + 1, :].to_broadcast([P, KVR])).then_inc(qkvg_loaded, 16)
            pool.dma_start(relx[0:BUCKETS, :], A["rel_bias"]).then_inc(rel_loaded, 16)
            pool.dma_start(onehot[:], A["c_onehot"]).then_inc(rel_loaded, 16)
            if "ssd" in kinds:
                for n, (dst, src) in enumerate((
                        (crows[0:80, :], A["ssd_conv_w"][0].rearrange("k (t p) -> (k t) p", p=P)),
                        (crows[80:100, :], A["ssd_conv_b"][0].rearrange("(t p) -> t p", p=P)),
                        (crows[100:116, :], A["ssd_norm"][0].rearrange("(t p) -> t p", p=P)),
                        (drow[:], A["ssd_d"][0].rearrange("(t a) -> t a", a=2)),
                        (headc[:, 0:1], A["ssd_dt_bias"][0].unsqueeze(1)),
                        (headc[:, 1:2], A["ssd_a_log"][0].unsqueeze(1)))):
                    pool.dma_start(dst, src).then_inc(ssd_loaded, 16)
                pool.dma_start(upper[:], A["c_upper"]).then_inc(upper_loaded, 16)
            if "moba" in kinds:
                pool_bias_store(pool)
            for j in range(NN):
                if j in norm_index:
                    pool_norm(pool, j)
                if j < NN - 1 and stages[j][0] == "moba":
                    pool_bias_load(pool, j)
                if j < NN - 1 and stages[j][0] == "ssd":
                    pool_ssd(pool, j, stages[j][1])
                if j < NN - 1 and stages[j][0] == "mla":
                    pool_mla(pool, stages[j][1], stages[j][2])

        @block.scalar
        def _(act):
            act_angles(act)
            for j, (kind, L, i) in enumerate(stages):
                act_norm(act, j)
                if kind == "mlp":
                    act_mlp(act, j, L)
                if kind == "ssd":
                    act_ssd(act, j, L)
                if kind == "mla":
                    act_mla(act, j, L, i)
                if kind == "moba":
                    act_moba(act, j, L)
            act_sumsq(act, NN - 1)

        @block.vector
        def _(dve):
            dve_angles(dve)
            if "moba" in kinds:
                dve_bias(dve)
            dve.wait_ge(consts, 32)
            for j in range(NN):
                deferred = j < NN - 1 and stages[j][0] == "mlp"
                for t in range(T):
                    if j:
                        dve_residual(dve, j - 1, t)
                    dve_scale_x(dve, j, t, deferred)
                if j == NN - 1:
                    break
                kind, L, i = stages[j]
                dve_norm_lo(dve, j)
                if kind == "mlp":
                    dve_mlp(dve, j, L)
                if kind == "ssd":
                    dve_ssd(dve, j, L)
                if kind == "mla":
                    dve_mla(dve, j, L, i)
                if kind == "moba":
                    dve_moba(dve, j, L)

        @block.tensor
        def _(te):
            te.wait_ge(consts, 32)
            if "moba" in kinds:
                pe_bias(te)
            for j, (kind, L, i) in enumerate(stages):
                pe_norm(te, j)
                if kind == "mlp":
                    pe_mlp(te, j, L)
                if kind == "ssd":
                    pe_ssd(te, j, L)
                if kind == "mla":
                    pe_mla(te, j, L)
                if kind == "moba":
                    pe_moba(te, j, L)


_STAGES = [("mla", 0, 0), ("mlp", 0, 0), ("moba", 1, 0), ("mlp", 1, 0), ("ssd", 2, 0), ("mlp", 2, 0), ("mla", 3, 1),
           ("mlp", 3, 0)]


def kernel(**inputs):
    import concourse.bacc as _bacc
    from concourse.bass_utils import run_bass_kernel_spmd as _run

    nc = _bacc.Bacc("TRN2", target_bir_lowering=False, num_devices=1)
    arrays, args = {}, {}
    for name, a in {**inputs, **shape_constants()}.items():
        a = np.ascontiguousarray(a)
        arrays[f"in_{name}"] = a
        args[name] = nc.dram_tensor(f"in_{name}", a.shape, mybir.dt.from_np(a.dtype), kind="ExternalInput").ap()
    out = nc.dram_tensor("out_0", (1, SEQ, DM), F32, kind="ExternalOutput").ap()
    build(nc, args, out, _STAGES)
    return _run(nc, [arrays], core_ids=[0]).results[0]["out_0"]
```
